# Optimizing a Trainium2 kernel written in Bass

```python
import math
import jax, jax.numpy as jnp
from jax import lax
import numpy as np

D_MODEL = 2048
BATCH = 1
SEQ = 256
DEPTH = 2

GRID_W = 64
CTX_LEN = 256
N_MIXERS = 2
EPS = 1e-6
GLA_HEADS = 4
GLA_KEY_DIM = D_MODEL // 2
GLA_VAL_DIM = D_MODEL
GLA_DK = GLA_KEY_DIM // GLA_HEADS
GLA_DV = GLA_VAL_DIM // GLA_HEADS
GLA_GATE_RANK = 16
GLA_GATE_NORM = 16.0
GLA_CHUNK = 64
GLA_IN_DIM = 2 * GLA_KEY_DIM + 2 * GLA_VAL_DIM
DIFF_HEAD_DIM = 128
DIFF_HEADS = D_MODEL // (2 * DIFF_HEAD_DIM)
DIFF_VAL_DIM = 2 * DIFF_HEAD_DIM
DIFF_WIDTH = DIFF_HEADS * DIFF_VAL_DIM
DIFF_IN_DIM = 4 * DIFF_WIDTH
Q_BLOCK = 128
ROPE_BASE = 10000.0

kernel_name = "hybrid_gla_diffattn_prefix_dit"

def rmsnorm(x, w):
    xf = x.astype(jnp.float32)
    y = xf * lax.rsqrt(jnp.mean(xf * xf, axis=-1, keepdims=True) + EPS)
    return (y * w.astype(jnp.float32)).astype(x.dtype)

def adaln(cond, w, b):
    m = jax.nn.silu(cond) @ w + b
    return jnp.split(m, 3, axis=-1)

def axial_rope_tables(n_tokens):
    rows_n = n_tokens // GRID_W
    row = jnp.repeat(jnp.arange(rows_n), GRID_W).astype(jnp.float32)
    col = jnp.tile(jnp.arange(GRID_W), rows_n).astype(jnp.float32)
    half = DIFF_HEAD_DIM // 2
    inv_freq = ROPE_BASE ** (-jnp.arange(0, half, 2, dtype=jnp.float32) / half)
    ang_r = row[:, None] * inv_freq
    ang_c = col[:, None] * inv_freq
    ang = jnp.concatenate([ang_r, ang_r, ang_c, ang_c], axis=-1)
    return jnp.cos(ang), jnp.sin(ang)

def apply_axial_rope(t, cos, sin):
    q4 = DIFF_HEAD_DIM // 4
    x1, x2, x3, x4 = t[..., :q4], t[..., q4:2 * q4], t[..., 2 * q4:3 * q4], t[..., 3 * q4:]
    rot = jnp.concatenate([-x2, x1, -x4, x3], axis=-1)
    cb = cos[None, :, None, None, :]
    sb = sin[None, :, None, None, :]
    return (t * cb + rot * sb).astype(t.dtype)

def gla_scan(q, k, v, log_a, s0):
    b_, t_, h_, _ = q.shape
    dv = v.shape[-1]
    n = t_ // GLA_CHUNK

    def chunks(t):
        return t.astype(jnp.float32).reshape(b_, n, GLA_CHUNK, h_, t.shape[-1]).transpose(1, 0, 3, 2, 4)

    lower = jnp.tril(jnp.ones((GLA_CHUNK, GLA_CHUNK), dtype=bool))

    def step(S, inp):
        qc, kc, vc, ac = inp
        bcum = jnp.cumsum(ac, axis=-2)
        o_inter = jnp.einsum('bhid,bhde->bhie', qc * jnp.exp(bcum), S)
        rel = bcum[:, :, :, None, :] - bcum[:, :, None, :, :]
        decay = jnp.exp(jnp.where(lower[:, :, None], rel, -jnp.inf))
        scores = jnp.einsum('bhid,bhjd,bhijd->bhij', qc, kc, decay)
        o_intra = jnp.einsum('bhij,bhje->bhie', scores, vc)
        b_last = bcum[:, :, -1:, :]
        S_new = jnp.exp(b_last[:, :, 0, :])[..., None] * S + jnp.einsum(
            'bhjd,bhje->bhde', kc * jnp.exp(b_last - bcum), vc)
        return S_new, o_inter + o_intra

    s_fin, o = lax.scan(step, s0, (chunks(q), chunks(k), chunks(v), chunks(log_a)))
    o = o.transpose(1, 0, 3, 2, 4).reshape(b_, t_, h_, dv)
    return o, s_fin

def gla_bidir(q, k, v, la_f, la_b, s0_f, s0_b):
    o_f, s_f = gla_scan(q, k, v, la_f, s0_f)
    fl = lambda t: jnp.flip(t, axis=1)
    o_b, s_b = gla_scan(fl(q), fl(k), fl(v), fl(la_b), s0_b)
    return o_f + fl(o_b), s_f, s_b

def gla_mixer(h, hc, w_in, gate_a1, gate_a2, gate_b, gn_w, w_out, need_ctx):
    def project(t):
        bt, tt = t.shape[:2]
        p = t @ w_in
        q, k, v, g = jnp.split(p, [GLA_KEY_DIM, 2 * GLA_KEY_DIM, 2 * GLA_KEY_DIM + GLA_VAL_DIM], axis=-1)
        q = q.reshape(bt, tt, GLA_HEADS, GLA_DK) * (GLA_DK ** -0.5)
        k = k.reshape(bt, tt, GLA_HEADS, GLA_DK)
        v = v.reshape(bt, tt, GLA_HEADS, GLA_DV)
        tf = t.astype(jnp.float32)
        las = [(jax.nn.log_sigmoid((tf @ gate_a1[d]) @ gate_a2[d] + gate_b[d]) / GLA_GATE_NORM
                ).reshape(bt, tt, GLA_HEADS, GLA_DK) for d in range(2)]
        return q, k, v, g, las[0], las[1]

    def finish(o, g):
        bt, tt = o.shape[:2]
        o = rmsnorm(o, gn_w).reshape(bt, tt, GLA_VAL_DIM).astype(g.dtype)
        return (o * jax.nn.silu(g)) @ w_out

    b_ = h.shape[0]
    zeros = jnp.zeros((b_, GLA_HEADS, GLA_DK, GLA_DV), jnp.float32)
    qc, kc, vc, gc, lafc, labc = project(hc)
    o_c, s_f, s_b = gla_bidir(qc, kc, vc, lafc, labc, zeros, zeros)
    q, k, v, g, laf, lab = project(h)
    o, _, _ = gla_bidir(q, k, v, laf, lab, s_f, s_b)
    y = finish(o, g)
    yc = finish(o_c, gc) if need_ctx else None
    return y, yc

def diff_attend(qb, k_all, v_all, lam):
    s = jnp.einsum('bqhmd,bkhmd->bhmqk', qb, k_all) * (DIFF_HEAD_DIM ** -0.5)
    p = jax.nn.softmax(s, axis=-1)
    a = p[:, :, 0] - lam * p[:, :, 1]
    return jnp.einsum('bhqk,bkhe->bqhe', a, v_all)

def diff_mixer(h, hc, w_in, qn_w, kn_w, lam_v, subln_w, w_out, lambda_init, cos, sin, need_ctx):
    def project(t):
        bt, tt = t.shape[:2]
        q, k, v, g = jnp.split(t @ w_in, 4, axis=-1)
        q = rmsnorm(q.reshape(bt, tt, DIFF_HEADS, 2, DIFF_HEAD_DIM), qn_w)
        k = rmsnorm(k.reshape(bt, tt, DIFF_HEADS, 2, DIFF_HEAD_DIM), kn_w)
        v = v.reshape(bt, tt, DIFF_HEADS, DIFF_VAL_DIM)
        return q, k, v, g

    lv = lam_v.astype(jnp.float32)
    lam = jnp.exp(jnp.sum(lv[0] * lv[1])) - jnp.exp(jnp.sum(lv[2] * lv[3])) + lambda_init

    q, k, v, g = project(h)
    q = apply_axial_rope(q, cos, sin)
    k = apply_axial_rope(k, cos, sin)
    qc, kc, vc, gc = project(hc)
    f32 = jnp.float32
    k_all = jnp.concatenate([k, kc], axis=1).astype(f32)
    v_all = jnp.concatenate([v, vc], axis=1).astype(f32)

    b_, s_ = h.shape[:2]
    nblk = s_ // Q_BLOCK
    q_blocks = q.astype(f32).reshape(b_, nblk, Q_BLOCK, DIFF_HEADS, 2, DIFF_HEAD_DIM).transpose(1, 0, 2, 3, 4, 5)
    o = lax.map(lambda qb: diff_attend(qb, k_all, v_all, lam), q_blocks)
    o = o.transpose(1, 0, 2, 3, 4).reshape(b_, s_, DIFF_HEADS, DIFF_VAL_DIM)

    def finish(o, g):
        bt, tt = o.shape[:2]
        o = (rmsnorm(o, subln_w) * (1.0 - lambda_init)).reshape(bt, tt, DIFF_WIDTH).astype(g.dtype)
        return (o * jax.nn.silu(g)) @ w_out

    y = finish(o, g)
    yc = None
    if need_ctx:
        o_c = diff_attend(qc.astype(f32), kc.astype(f32), vc.astype(f32), lam)
        yc = finish(o_c, gc)
    return y, yc

def setup_inputs(seed: int = 0) -> dict:
    key = jax.random.key(seed)
    ks = jax.random.split(key, 24)
    n_a = (DEPTH + N_MIXERS - 1) // N_MIXERS
    n_b = DEPTH // N_MIXERS
    nrm = jax.random.normal
    f32 = jnp.float32
    D = D_MODEL
    return {
        "x": nrm(ks[0], (BATCH, SEQ, D), f32),
        "c": nrm(ks[1], (BATCH, D), f32),
        "ctx": nrm(ks[2], (BATCH, CTX_LEN, D), f32),
        "c_ctx": nrm(ks[3], (D,), f32),
        "norm_w": 1.0 + 0.02 * nrm(ks[4], (DEPTH, D), f32),
        "ada_w": nrm(ks[5], (DEPTH, D, 3 * D), f32) * D ** -0.5,
        "ada_b": 0.02 * nrm(ks[6], (DEPTH, 3 * D), f32),
        "gla_w_in": nrm(ks[7], (n_a, D, GLA_IN_DIM), f32) * D ** -0.5,
        "gla_gate_a1": nrm(ks[8], (n_a, 2, D, GLA_GATE_RANK), f32) * D ** -0.5,
        "gla_gate_a2": nrm(ks[9], (n_a, 2, GLA_GATE_RANK, GLA_KEY_DIM), f32) * GLA_GATE_RANK ** -0.5,
        "gla_gate_b": 0.1 * nrm(ks[10], (n_a, 2, GLA_KEY_DIM), f32),
        "gla_gn_w": 1.0 + 0.02 * nrm(ks[11], (n_a, GLA_DV), f32),
        "gla_w_out": nrm(ks[12], (n_a, GLA_VAL_DIM, D), f32) * GLA_VAL_DIM ** -0.5,
        "diff_w_in": nrm(ks[13], (n_b, D, DIFF_IN_DIM), f32) * D ** -0.5,
        "diff_qn_w": 1.0 + 0.02 * nrm(ks[14], (n_b, 2, DIFF_HEAD_DIM), f32),
        "diff_kn_w": 1.0 + 0.02 * nrm(ks[15], (n_b, 2, DIFF_HEAD_DIM), f32),
        "diff_lam": 0.1 * nrm(ks[16], (n_b, 4, DIFF_HEAD_DIM), f32),
        "diff_subln_w": 1.0 + 0.02 * nrm(ks[17], (n_b, DIFF_VAL_DIM), f32),
        "diff_w_out": nrm(ks[18], (n_b, DIFF_WIDTH, D), f32) * DIFF_WIDTH ** -0.5,
    }

def reference(x, c, ctx, c_ctx, norm_w, ada_w, ada_b,
              gla_w_in, gla_gate_a1, gla_gate_a2, gla_gate_b, gla_gn_w, gla_w_out,
              diff_w_in, diff_qn_w, diff_kn_w, diff_lam, diff_subln_w, diff_w_out):
    cos, sin = axial_rope_tables(x.shape[1])
    for i in range(DEPTH):
        last = i == DEPTH - 1
        j = i // N_MIXERS
        shift, scale, gate = adaln(c, ada_w[i], ada_b[i])
        shift_c, scale_c, gate_c = adaln(c_ctx, ada_w[i], ada_b[i])
        h = rmsnorm(x, norm_w[i]) * (1.0 + scale[:, None]) + shift[:, None]
        hc = rmsnorm(ctx, norm_w[i]) * (1.0 + scale_c) + shift_c
        if i % N_MIXERS == 0:
            y, yc = gla_mixer(h, hc, gla_w_in[j], gla_gate_a1[j], gla_gate_a2[j], gla_gate_b[j],
                              gla_gn_w[j], gla_w_out[j], not last)
        else:
            lambda_init = 0.8 - 0.6 * math.exp(-0.3 * i)
            y, yc = diff_mixer(h, hc, diff_w_in[j], diff_qn_w[j], diff_kn_w[j], diff_lam[j],
                               diff_subln_w[j], diff_w_out[j], lambda_init, cos, sin, not last)
        x = x + gate[:, None] * y
        if not last:
            ctx = ctx + gate_c * yc
    return x


_drawn_inputs = setup_inputs


def setup_inputs(seed=0):
    import zlib

    import numpy as np

    out = dict(_drawn_inputs(seed))
    spreads = {}
    factors = {'norm_w': 3.164,
     'gla_gn_w': 5.721,
     'diff_qn_w': 8.0,
     'diff_kn_w': 8.0,
     'diff_subln_w': 8.0}
    for name, (base, spread) in spreads.items():
        noise = np.random.default_rng([zlib.crc32(name.encode()), seed]).standard_normal(out[name].shape)
        drawn = base * np.exp(spread * noise) if base else spread * noise
        out[name] = __import__('jax').numpy.asarray(drawn.astype(out[name].dtype))
    for name, factor in factors.items():
        out[name] = (out[name] * factor).astype(out[name].dtype)
    return out
```

```python
import math
from contextlib import ExitStack

import numpy as np

import concourse.bass as bass
from concourse import mybir

F32 = mybir.dt.float32
F32R = mybir.dt.float32r
I32 = mybir.dt.int32
ACT = mybir.ActivationFunctionType
ALU = mybir.AluOpType
AX = mybir.AxisListType

P = 128
D = 2048
NT = 4
TOK = NT * P
X0, X1, C0, C1 = range(NT)
NK = D // P
CW = 512
PAIRS = NK // 2
RING = 4
EPS = 1e-6
GRID_W = 64
ROPE_BASE = 10000.0

G_HEADS, G_DK, G_DV, G_RANK = 4, 256, 512, 16
G_NORM = 16.0
HALF = 64
A_HEADS, A_D, A_DV = 8, 128, 256
LAMBDA_INIT = 0.8 - 0.6 * math.exp(-0.3)

OUT0 = 3 * G_HEADS
DIFF = OUT0 + 4
OUT1 = DIFF + 2 * A_HEADS
CHUNKS = OUT1 + 4
STARTUP = 8

V_C, V_CCTX, V_NORM, V_GATEB, V_GN, V_LAM, V_SUB, V_ROWS = 0, 16, 32, 64, 80, 84, 88, 90


class Steps:

    def __init__(self, eng, sem):
        self.eng, self.sem, self.base, self.n = eng, sem, 0, 0

    def step(self, ins):
        ins.then_inc(self.sem, 1)
        self.n += 1

    def wait(self):
        self.eng.wait_ge(self.sem, self.base + self.n)

    def enter(self, i, per):
        self.start, self.per = self.base + self.n, per
        self.base, self.n = i * per + self.start, 0

    def leave(self, rounds):
        assert self.n == self.per, f"{self.n} steps in a round, not {self.per}"
        self.base, self.n = self.start + rounds * self.per, 0


def build(nc, io, out):
    with ExitStack() as ctx:
        def sb(name, shape, dt=F32):
            return ctx.enter_context(nc.sbuf_tensor(name, shape, dt))

        def sem(name):
            return ctx.enter_context(nc.semaphore(name))

        hi = sb("acts_hi", [P, NK, TOK], F32R)
        lo = sb("acts_lo", [P, NK, TOK], F32R)
        w_hi = sb("w_hi", [P, RING, 2, CW], F32R)
        w_lo = sb("w_lo", [P, RING, 2, CW], F32R)
        a1_hi = sb("a1_hi", [P, NK, 2 * G_RANK], F32R)
        a1_lo = sb("a1_lo", [P, NK, 2 * G_RANK], F32R)
        raw = sb("w_raw", [P, RING, 2, CW])
        ada_w = sb("ada_w", [P, 2, CW])
        u = sb("u", [P, NT, D])
        work = sb("work", [P, 10752])
        ident = sb("ident_sb", [P, P])
        ones = sb("ones", [P, P])
        mask1 = sb("mask1_sb", [P, P], I32)
        mask2 = sb("mask2_sb", [P, HALF], I32)
        zT = sb("gate_zT", [48, TOK])
        a2 = sb("gate_a2", [48, G_DK])
        cols1 = sb("cols1", [P, V_ROWS])
        cols2 = sb("cols2", [P, 96])
        silu_c = sb("silu_c", [P, NK, 2])
        mod = sb("mod", [P, 6, NK, 2])
        d1m = sb("d1m", [P, NT, P])
        d2m = sb("d2m", [P, NT, P])
        g_tot = sb("g_tot", [P, NT])
        stat = sb("stat", [P, 4, 8])
        smx = sb("softmax_stat", [P, 4, 4])
        lam = sb("lam", [P, 8])

        def view(at, *shape):
            n = int(np.prod(shape))
            v = work[:, at:at + n]
            if len(shape) == 1:
                return v
            names = "abcd"[:len(shape)]
            kw = {names[i]: shape[i] for i in range(1, len(shape))}
            return v.rearrange(f"p ({' '.join(names)}) -> p {' '.join(names)}", **kw)

        xn = view(0, NT, D)
        hf = view(NT * D, 2, TOK)
        a1_raw = view(NT * D + 2 * TOK, NK, 2 * G_RANK)
        vec1 = view(9728, P)
        vec2 = view(9856, P)
        lam_pr = view(9984, 2)
        qkT = view(0, 4, TOK)
        v_sb = view(2048, NT, CW)
        bcum = view(4096, 4, TOK)
        silu_g = view(4096, NT, CW)
        t0 = 6144
        ln_t = view(t0, 4, TOK)
        qh = view(t0, TOK)
        kb = view(t0 + 512, TOK)
        q2 = view(t0 + 1024, TOK)
        k2 = view(t0 + 1536, TOK)
        q1 = view(t0 + 2048, NT, HALF)
        k1 = view(t0 + 2304, NT, HALF)
        qA = view(t0 + 2560, 2 * P)
        qB = view(t0 + 2816, 2 * P)
        o_sb = view(t0, NT, CW)
        o_sq = view(t0 + 2048, CW)
        z_sb = view(t0 + 2560, NT, 2 * G_RANK)
        at = view(t0 + 3072, 3, CW)
        gate_row = view(0, 2, D)
        xres = view(4096, NT, CW)
        yrow = view(6144, NT, CW)
        diag4 = view(8192, 4, P)
        hfu = view(8704, 2, TOK)
        rope = view(0, 4, 2, 256)
        knw = view(2048, 256)
        silu_ag = view(2304, 2, A_DV)
        kv = view(2816, NT, CW)
        qg = view(4864, 2, CW)
        kT = view(5888, 2, TOK)
        qT = view(6912, 2, 2 * P)
        probs = view(7424, 2, 2, CW)
        k_n = view(7424, NT, 256)
        k_t = view(8448, NT, 256)
        aT = view(9472, NT, 2 * P)
        q_t = view(9472, 2, 256)
        q_u = view(9984, 2, 256)
        o1 = q_t
        u1 = u[:, 2:4, :]

        bank = [ctx.enter_context(nc.psum_tensor(f"bank{i}", [P, CW], F32)) for i in range(8)]

        vec_in, const_in, x_in, a1_in, a2_in = (sem(n) for n in ("vec_in", "const_in", "x_in", "a1_in", "a2_in"))
        raw_in = [sem(f"raw_in{i}") for i in range(RING)]
        ada_in = [sem(f"ada_in{i}") for i in range(2)]
        xres_in = sem("xres_in")
        rows_in = sem("rows_in")
        rope_ok = sem("rope_ok")
        cols_t = sem("cols_t")
        cols_ok = sem("cols_ok")
        silu_ok = sem("silu_ok")
        ada0_used = sem("ada0_used")
        ada_used = sem("ada_used")
        ada_taken = sem("ada_taken")
        w_hi_ok = sem("w_hi_ok")
        w_split = sem("w_split")
        pair_done = sem("pair_done")
        acc_ok = sem("acc_ok")
        freed = [sem(f"freed{i}") for i in range(NT)]
        sq_ok = sem("sq_ok")
        mean_ok = sem("mean_ok")
        rs_ok = sem("rs_ok")
        xn_ok = sem("xn_ok")
        xt_ok = sem("xt_ok")
        hf_ok = sem("hf_ok")
        hi_ok = sem("hi_ok")
        acts_ok = sem("acts_ok")
        a1_hi_ok, a1_ok, z_ok, z_sb_ok, zt_ok, zT_ok = (
            sem(n) for n in ("a1_hi_ok", "a1_ok", "z_ok", "z_sb_ok", "zt_ok", "zT_ok"))
        logit_ok = sem("logit_ok")
        logit_out = sem("logit_out")
        ln_ok = sem("ln_ok")
        d_ok = sem("d_ok")
        e_ok = sem("e_ok")
        til_ok = sem("til_ok")
        unit_done = sem("unit_done")
        at_ok = sem("at_ok")
        o_ok = sem("o_ok")
        o_out = sem("o_out")
        g_ok = sem("g_ok")
        u_ok = sem("u_ok")
        diag_ok, gate_t, gate_ok = sem("diag_ok"), sem("gate_t"), sem("gate_ok")
        x1_ok = sem("x1_ok")
        k_ok = sem("k_ok")
        kt_t = sem("kt_t")
        kT_ok = sem("kT_ok")
        q_ok = sem("q_ok")
        qt_t = sem("qt_t")
        qT_ok = sem("qT_ok")
        s_ok = sem("s_ok")
        max_ok = sem("max_ok")
        p_ok = sem("p_ok")
        a_ok = sem("a_ok")
        at_t = sem("at_t")
        aT_ok = sem("aT_ok")
        pv_ok = sem("pv_ok")
        lam_t, lam_pr_ok, lam_e, lam_ok = sem("lam_t"), sem("lam_pr_ok"), sem("lam_e"), sem("lam_ok")
        y_ok = sem("y_ok")
        y_out = sem("y_out")
        dve_step = sem("dve_step")
        act_step = sem("act_step")

        block = ctx.enter_context(nc.Block())

        @block.sync
        def _(sp):
            for dst, src in (
                (vec1[V_C:V_C + NK], io["c"].rearrange("o (k p) -> (o k) p", p=P)),
                (vec1[V_CCTX:V_CCTX + NK], io["c_ctx"].rearrange("(k p) -> k p", p=P)),
                (vec1[V_NORM:V_NORM + 2 * NK], io["norm_w"].rearrange("l (k p) -> (l k) p", p=P)),
                (vec1[V_GATEB:V_GATEB + 16], io["gla_gate_b"].rearrange("o d (k p) -> (o d k) p", p=P)),
                (vec1[V_GN:V_GN + 4], io["gla_gn_w"].rearrange("o (k p) -> (o k) p", p=P)),
                (vec1[V_LAM:V_LAM + 4], io["diff_lam"].rearrange("o r p -> (o r) p")),
                (vec1[V_SUB:V_SUB + 2], io["diff_subln_w"].rearrange("o (k p) -> (o k) p", p=P)),
                (vec2[0:96], io["ada_b"].rearrange("l (k p) -> (l k) p", p=P)),
            ):
                sp.dma_start(dst, src).then_inc(vec_in, 16)
            for dst, src in ((ident[:], io["ident"]), (mask1[:], io["mask1"]), (mask2[:], io["mask2"])):
                sp.dma_start(dst, src).then_inc(const_in, 16)
            sp.sem_inc(w_split, RING)
            sp.sem_inc(pair_done, RING)
            sp.sem_inc(ada_used, 2)

            aw0 = io["ada_w"][0].rearrange("(k p) n -> p k n", p=P)
            aw1 = io["ada_w"][1].rearrange("(k p) n -> p k n", p=P)

            def startup_chunk(a, first):
                for p in range(PAIRS):
                    if not (first and p < RING):
                        sp.wait_ge(ada0_used, a * PAIRS + (p - RING + 1))
                    sp.dma_start(raw[:, p % RING], aw0[:, 2 * p:2 * p + 2, bass.ds(a * CW, CW)])\
                        .then_inc(raw_in[p % RING], 16)

            startup_chunk(0, True)
            for t in range(NT):
                src = io["x"][0] if t < C0 else io["ctx"][0]
                sp.dma_start(u[:, t, :], src[(t % 2) * P:(t % 2 + 1) * P, :]).then_inc(x_in, 16)
            for dr in range(2):
                sp.dma_start(a1_raw[:, :, dr * G_RANK:(dr + 1) * G_RANK],
                             io["gla_gate_a1"][0, dr].rearrange("(k p) r -> p k r", p=P)).then_inc(a1_in, 16)
            with sp.Fori(1, STARTUP) as a:
                startup_chunk(a, False)
            sp.wait_ge(ada0_used, STARTUP * PAIRS)

            def load_pair(c, p, parts):
                moves = parts(p)
                sp.wait_ge(w_split, c * PAIRS + (p + 1))
                for dst, src in moves:
                    sp.dma_start(dst, src).then_inc(raw_in[p % RING], 16)

            def side_by_side(w, first, second):
                n = CW // 2

                def parts(p):
                    slot = raw[:, p % RING]
                    return [(slot[:, :, n:CW], w[:, 2 * p:2 * p + 2, bass.ds(second, n)]),
                            (slot[:, :, 0:n], w[:, 2 * p:2 * p + 2, bass.ds(first, n)])]
                return parts

            def one_range(w, first):
                def parts(p):
                    return [(raw[:, p % RING, j], w[:, 2 * p + j, bass.ds(first, CW)]) for j in range(2)]
                return parts

            def load_chunk(c, parts, following, ada_from=None):
                for p in range(PAIRS):
                    if p < RING:
                        load_pair(c, p + RING, parts)
                    elif following is not None:
                        load_pair(c + 1, p - RING, following)
                    if ada_from is not None:
                        for k in (2 * p, 2 * p + 1):
                            sp.wait_ge(ada_used, c * NK + (k + 1))
                            sp.dma_start(ada_w[:, k % 2], ada_from[0][:, k, bass.ds(ada_from[1], CW)])\
                                .then_inc(ada_in[k % 2], 16)

            wg = io["gla_w_in"][0].rearrange("(k p) n -> p k n", p=P)
            wo = io["gla_w_out"][0].rearrange("(k p) n -> p k n", p=P)
            wd = io["diff_w_in"][0].rearrange("(k p) n -> p k n", p=P)
            w1 = io["diff_w_out"][0].rearrange("(k p) n -> p k n", p=P)
            key0, val0, gate0 = 1024, 2048, 4096

            def q_and_k(h):
                return side_by_side(wg, h * G_DK, h * G_DK + key0)

            def gla_head(h, following):
                if not (isinstance(h, int) and h == 0):
                    sp.wait_ge(logit_ok, h * 4)
                for dr in range(2):
                    sp.dma_start(a2[32 * dr:32 * dr + G_RANK, :],
                                 io["gla_gate_a2"][0, dr][:, bass.ds(h * G_DK, G_DK)]).then_inc(a2_in, 16)
                c = h * 3
                v, g = one_range(wg, h * G_DV + val0), one_range(wg, h * G_DV + gate0)
                load_chunk(c, q_and_k(h), v, (aw0, h * CW + 2 * D))
                load_chunk(c + 1, v, g, (aw1, h * CW))
                load_chunk(c + 2, g, following, (aw1, h * CW + D))

            def out0(j, following):
                load_chunk(j + OUT0, one_range(wo, j * CW), following, (aw1, j * CW + 2 * D))

            def k_and_v(h):
                return side_by_side(wd, h * A_DV + D, h * A_DV + 2 * D)

            def attention_head(h, following):
                c = h * 2 + DIFF
                q_and_g = side_by_side(wd, h * A_DV, h * A_DV + 3 * D)
                load_chunk(c, k_and_v(h), q_and_g)
                load_chunk(c + 1, q_and_g, following)

            for p in range(RING):
                load_pair(0, p, q_and_k(0))
            gla_head(0, q_and_k(1))
            with sp.Fori(1, G_HEADS - 1) as h:
                gla_head(h, q_and_k(h + 1))
            gla_head(G_HEADS - 1, one_range(wo, 0))
            with sp.Fori(0, 3) as j:
                out0(j, one_range(wo, (j + 1) * CW))
            out0(3, k_and_v(0))
            with sp.Fori(0, A_HEADS - 1) as h:
                attention_head(h, k_and_v(h + 1))
            attention_head(A_HEADS - 1, one_range(w1, 0))
            with sp.Fori(0, 3) as j:
                load_chunk(j + OUT1, one_range(w1, j * CW), one_range(w1, (j + 1) * CW))
            load_chunk(CHUNKS - 1, one_range(w1, 3 * CW), None)

        @block.gpsimd
        def _(pool):
            pool.memset(ones[:], 1.0).then_inc(const_in, 1)
            pool.memset(d1m[:], 0.0).then_inc(const_in, 1)
            pool.memset(d2m[:], 0.0).then_inc(const_in, 1)
            with pool.Fori(0, CHUNKS) as c:
                for p in range(PAIRS):
                    pool.wait_ge(w_hi_ok, c * PAIRS + (p + 1))
                    pool.tensor_tensor(w_lo[:, p % RING], raw[:, p % RING], w_hi[:, p % RING].bitcast(F32),
                                       ALU.subtract).then_inc(w_split, 1)

        CONSTS = 3 * 16 + 3

        @block.scalar
        def _(act):
            st = Steps(act, act_step)

            def split(c, p):
                act.wait_ge(raw_in[p % RING], c * 64 + (16 * 2 * STARTUP + 32 * (p // RING + 1)))
                act.wait_ge(pair_done, c * PAIRS + (p + 1))
                act.activation(w_hi[:, p % RING], raw[:, p % RING], ACT.Copy).then_inc(w_hi_ok, 1)

            def splits(c, ps):
                for p in ps:
                    split(c, p)

            def rsqrt(n, width):
                act.wait_ge(mean_ok, n)
                st.step(act.activation(stat[:, 3, 0:width], stat[:, 1, 0:width], ACT.Ln))
                st.wait()
                act.activation(stat[:, 2, 0:width], stat[:, 3, 0:width], ACT.Exp, scale=-0.5).then_inc(rs_ok, 1)

            def row_squares():
                for t in range(NT):
                    act.activation(xn[:, t, :], u[:, t, :], ACT.Square, accum_out=stat[:, 0, t:t + 1])\
                        .then_inc(sq_ok, 1)

            def high_parts(stage, src, c):
                n = NT if stage < 3 else 2
                for k in range(NK):
                    if k >= 4 and k % 2 == 0 and k < 12:
                        split(c, k // 2 + 2)
                    act.wait_ge(hf_ok, stage * NK + k + 1)
                    act.activation(hi[:, k, 0:n * P], src[:, k % 2, 0:n * P], ACT.Copy).then_inc(hi_ok, 1)

            act.wait_ge(cols_ok, 1)
            for m in range(2):
                act.activation(silu_c[:, :, m], cols1[:, m * NK:(m + 1) * NK], ACT.Silu).then_inc(silu_ok, 1)
            act.wait_ge(lam_t, 1)
            act.activation(lam[:, 0:2], bank[4][:, 0:2], ACT.Exp).then_inc(lam_e, 1)
            act.wait_ge(a1_in, 32)
            act.activation(a1_hi[:], a1_raw, ACT.Copy).then_inc(a1_hi_ok, 1)
            act.wait_ge(x_in, 16 * NT)
            row_squares()
            rsqrt(1, NT)
            splits(0, range(4))
            high_parts(0, hf, 0)

            def decays(h, n):
                b = bcum[:, n, :]
                act.wait_ge(d_ok, h * 4 + (n + 1))
                st.step(act.activation(k2, q2, ACT.Exp, scale=-1.0 / G_NORM))
                act.activation(qh, b, ACT.Exp, scale=1.0 / G_NORM)
                act.activation(kb, kb, ACT.Exp, scale=-1.0 / G_NORM)
                act.activation(q1, q1, ACT.Exp, scale=1.0 / G_NORM)
                act.activation(k1, k1, ACT.Exp, scale=-1.0 / G_NORM)
                last = 0 if n < 2 else P - 1
                act.activation(g_tot[:], b.rearrange("p (t s) -> p t s", s=P)[:, :, last], ACT.Exp,
                               scale=1.0 / G_NORM)
                st.wait()
                act.activation(q2, q2, ACT.Exp, scale=1.0 / G_NORM).then_inc(e_ok, 1)

            def gla_head(h, first):
                c = h * 3
                if not first:
                    splits(c, range(4, 8))
                splits(c + 1, range(0, 2))
                act.wait_ge(logit_out, h * 4 + 4)
                st.step(act.activation(ln_t, bcum, ACT.Abs))
                st.wait()
                st.step(act.activation(ln_t, ln_t, ACT.Exp, scale=-1.0))
                st.wait()
                act.activation(ln_t, ln_t, ACT.Ln, bias=1.0).then_inc(ln_ok, 1)
                splits(c + 1, range(2, 5))
                decays(h, 0)
                splits(c + 1, range(5, 8))
                decays(h, 1)
                splits(c + 2, range(0, 4))
                decays(h, 2)
                splits(c + 2, range(4, 6))
                decays(h, 3)
                splits(c + 2, range(6, 8))
                splits(c + 3, range(0, 4))
                for t in range(NT):
                    if t == NT - 1:
                        act.wait_ge(pair_done, c * PAIRS + (3 * PAIRS + RING))
                    else:
                        act.wait_ge(acc_ok, c * 3 + (6 + t + 1))
                    act.activation(silu_g[:, t], bank[t][:], ACT.Silu).then_inc(freed[t], 1)
                for t in range(NT):
                    act.wait_ge(o_out, h * 4 + (t + 1))
                    if t > 0:
                        act.wait_ge(sq_ok, h * NT + (NT + t))
                    act.activation(o_sq, o_sb[:, t], ACT.Square, accum_out=stat[:, 0, t:t + 1])\
                        .then_inc(sq_ok, 1)
                rsqrt(h + 2, NT)

            n0 = st.n
            gla_head(0, True)
            per = st.n - n0
            with act.Fori(1, G_HEADS) as h:
                st.enter(h - 1, per)
                gla_head(h, False)
                st.leave(G_HEADS - 1)

            def load_residual(j):
                act.wait_ge(x1_ok, j * NT)
                for t in range(NT):
                    src = io["x"][0] if t < C0 else io["ctx"][0]
                    act.dma_start(xres[:, t], src[(t % 2) * P:(t % 2 + 1) * P, bass.ds(j * CW, CW)])\
                        .then_inc(xres_in, 16)

            act.wait_ge(u_ok, NT * G_HEADS)
            load_residual(0)
            high_parts(1, hfu, OUT0)
            with act.Fori(1, 4) as j:
                splits(j + OUT0, range(4))
                load_residual(j)
                splits(j + OUT0, range(4, 8))
            splits(DIFF, range(4))
            act.wait_ge(x1_ok, 4 * NT)
            row_squares()
            rsqrt(G_HEADS + 2, NT)
            high_parts(2, hf, DIFF)

            def softmax(h):
                for i in range(4):
                    act.wait_ge(max_ok, h * 4 + (i + 1))
                    act.activation(probs[:, i // 2, i % 2], bank[4 + i][:], ACT.Exp, bias=smx[:, 0, i:i + 1],
                                   scale=A_D ** -0.5, accum_out=smx[:, 1, i:i + 1]).then_inc(p_ok, 1)

            BATCH = G_HEADS + 2

            def attention_head(h, before):
                c = h * 2 + DIFF
                if before:
                    splits(c, range(4, 7))
                    softmax(h - 1)
                    splits(c, range(7, 8))
                splits(c + 1, range(0, 3))
                if before:
                    rsqrt(h * 3 + BATCH, 2)
                splits(c + 1, range(3, 4))
                rsqrt(h * 3 + (BATCH + 1), 8)
                splits(c + 1, range(4, 8))
                splits(c + 2, range(0, 4))
                for t in range(2):
                    act.wait_ge(freed[t], h * 2 + (DIFF + 2))
                act.activation(silu_ag, qg[:, :, A_DV:CW], ACT.Silu).then_inc(g_ok, 1)
                rsqrt(h * 3 + (BATCH + 2), 4)

            act.wait_ge(acts_ok, 3 * NK)
            for i, name in enumerate(("cos", "sin", "cos", "sin")):
                act.dma_start(rope[:, i], io[name].rearrange("(t p) n -> p t n", p=P)).then_inc(rows_in, 16)
            act.dma_start(knw, io["diff_kn_w"][0].rearrange("m n -> (m n)").partition_broadcast(P))\
                .then_inc(rows_in, 16)
            act.dma_start(silu_ag[:, 0], io["diff_qn_w"][0].rearrange("m n -> (m n)").partition_broadcast(P))\
                .then_inc(rows_in, 16)
            act.wait_ge(rope_ok, 1)
            attention_head(0, False)
            with act.Fori(1, A_HEADS) as h:
                st.enter(h - 1, 3)
                attention_head(h, True)
                st.leave(A_HEADS - 1)
            softmax(A_HEADS - 1)
            rsqrt(A_HEADS * 3 + BATCH, 2)
            high_parts(3, hfu, OUT1)

            def store(j):
                act.wait_ge(y_ok, j * 2 + 2)
                for t in range(2):
                    act.dma_start(out[0][t * P:(t + 1) * P, bass.ds(j * CW, CW)], yrow[:, t]).then_inc(y_out, 16)

            with act.Fori(1, 4) as j:
                splits(j + OUT1, range(4))
                store(j - 1)
                splits(j + OUT1, range(4, 8))
            store(3)
            act.wait_ge(y_out, 4 * 2 * 16)

        @block.tensor
        def _(pe):
            def modulation_tile(w, k, first):
                for n in range(4):
                    last = pe.matmul(bank[7][:, 2 * n:2 * n + 2], w[:, n * P:(n + 1) * P], silu_c[:, k, :],
                                     start=(k == 0 and n == 0), stop=(k == NK - 1), skip_group_check=True)
                return last

            def background(c, k):
                pe.wait_ge(ada_in[k % 2], c * (8 * 16) + 16 * (k // 2 + 1))
                if k == 0:
                    pe.wait_ge(ada_taken, c + STARTUP)
                modulation_tile(ada_w[:, k % 2], k, c).then_inc(ada_used, 1)

            def project(c, frees, rows_stationary, tiles=NT, ada=None, before=None, after=None):
                for p in range(PAIRS):
                    if before is not None:
                        before(p)
                    pe.wait_ge(w_split, c * PAIRS + (p + 1 + RING))
                    for j in range(2):
                        k, wh, wl = 2 * p + j, w_hi[:, p % RING, j], w_lo[:, p % RING, j]
                        for t in range(tiles):
                            if k == 0:
                                pe.wait_ge(freed[t], frees(t))
                            x = slice(t * P, (t + 1) * P)
                            if rows_stationary:
                                ops = ((hi[:, k, x], wl), (hi[:, k, x], wh), (lo[:, k, x], wh))
                            else:
                                ops = ((wl[:, x], hi[:, k, :]), (wh[:, x], hi[:, k, :]), (wh[:, x], lo[:, k, :]))
                            for i, (a, b) in enumerate(ops):
                                last = pe.matmul(bank[t][:], a, b, start=(k == 0 and i == 0),
                                                 stop=(k == NK - 1 and i == 2))
                            if k == NK - 1 and t < tiles - 1:
                                last.then_inc(acc_ok, 1)
                        if j == 1:
                            last.then_inc(pair_done, 1)
                        if ada is not None:
                            background(ada, k)
                    if after is not None:
                        after(p)

            def transpose_tile(stage, src, k, n=NT):
                if k >= 3:
                    pe.wait_ge(hf_ok, stage * NK + k - 2)
                for t in range(n):
                    last = pe.transpose(bank[4 + k % 3][:, t * P:(t + 1) * P], src[:, t, k * P:(k + 1) * P], ident[:])
                last.then_inc(xt_ok, 1)

            def transposing(stage, src, n=NT):
                def before(p):
                    for k in range(0 if p == 0 else 2 * p + 2, min(2 * p + 4, NK)):
                        transpose_tile(stage, src, k, n)
                    pe.wait_ge(acts_ok, stage * NK + 2 * p + 2)
                return before

            pe.wait_ge(vec_in, 16 * 8)
            pe.wait_ge(const_in, CONSTS)
            pe.transpose(bank[4][:, 0:V_ROWS], vec1[0:V_ROWS, :], ident[0:V_ROWS, 0:V_ROWS]).then_inc(cols_t, 1)
            pe.transpose(bank[5][:, 0:96], vec2[0:96, :], ident[0:96, 0:96]).then_inc(cols_t, 1)
            pe.wait_ge(lam_pr_ok, 1)
            pe.matmul(bank[4][:, 0:2], ones[:], lam_pr, start=True, stop=True).then_inc(lam_t, 1)
            pe.wait_ge(silu_ok, 2)

            def startup_chunk(a, first):
                for p in range(PAIRS):
                    pe.wait_ge(raw_in[p % RING], a * 32 + 16 * (p // RING + 1))
                    for k in (2 * p, 2 * p + 1):
                        if k == 0 and not first:
                            pe.wait_ge(ada_taken, a)
                        last = modulation_tile(raw[:, p % RING, k % 2], k, a)
                    last.then_inc(ada0_used, 1)

            startup_chunk(0, True)
            with pe.Fori(1, STARTUP) as a:
                startup_chunk(a, False)

            def gate_columns():
                pe.wait_ge(a1_ok, 1)
                for t in range(NT):
                    for k in range(NK):
                        x = slice(t * P, (t + 1) * P)
                        for i, (a, b) in enumerate(((hi, a1_lo), (hi, a1_hi), (lo, a1_hi))):
                            last = pe.matmul(bank[4][:, t * 32:(t + 1) * 32], a[:, k, x], b[:, k, :],
                                             start=(k == 0 and i == 0), stop=(k == NK - 1 and i == 2))
                last.then_inc(z_ok, 1)
                pe.wait_ge(z_sb_ok, 1)
                for dr in range(2):
                    for t in range(NT):
                        last = pe.transpose(bank[5 + dr][0:G_RANK, t * P:(t + 1) * P],
                                            z_sb[:, t, dr * G_RANK:(dr + 1) * G_RANK], ident[:])
                    last.then_inc(zt_ok, 1)
                pe.wait_ge(zT_ok, 2)

            def gate_logits(h):
                pe.wait_ge(a2_in, h * 32 + 32)
                for n in range(4):
                    dr = 1 if n < 2 else 0
                    rows = slice(32 * dr, 32 * dr + G_RANK)
                    if n == 3:
                        pe.wait_ge(logit_out, h * 4 + 1)
                    elif n == 0:
                        pe.wait_ge(o_out, h * 4)
                    pe.matmul(bank[4 + n % 3][:], a2[rows, (n % 2) * P:(n % 2 + 1) * P], zT[rows, :],
                              start=True, stop=True).then_inc(logit_ok, 1)

            def score(out_, k_part, q_part, start=False):
                return pe.matmul(out_, k_part, q_part, start=start, stop=True, skip_group_check=True)

            DIAG = {X0: (6, 0), X1: (6, 384), C0: (4, 256), C1: (5, 384)}

            def tok(v, t, n=P, at_=0):
                return v[:, t * P + at_:t * P + at_ + n]

            def unit_scores(h, n):
                pe.wait_ge(til_ok, h * 4 + (n + 1))
                back, first = n < 2, n == 0
                score(bank[4][:, 0:256], tok(kb, C0), qB if back else qA, first)
                score(bank[5][:, 0:256], tok(kb, C1), qA if back else qB, first)
                if back:
                    score(bank[6][:, 256:384], tok(kb, X1), tok(qh, X0), first)
                    score(bank[5][:, 256:384], tok(kb, C1), tok(qh, C0))
                else:
                    score(bank[6][:, 128:256], tok(kb, X0), tok(qh, X1))
                    score(bank[4][:, 384:512], tok(kb, C0), tok(qh, C1))
                for t in range(NT):
                    b, at_ = DIAG[t]
                    low, high = slice(0, HALF), slice(HALF, P)
                    if back:
                        score(bank[b][high, at_:at_ + HALF], k1[:, t], q1[:, t])
                        col = 256 + t * HALF
                        score(bank[7][low, col:col + HALF], tok(k2, t, HALF), tok(q2, t, HALF))
                        last = score(bank[7][high, col:col + HALF], tok(k2, t, HALF, HALF), tok(q2, t, HALF, HALF))
                    else:
                        score(bank[b][low, at_ + HALF:at_ + P], k1[:, t], q1[:, t])
                        score(bank[b][low, at_:at_ + HALF], tok(k2, t, HALF), tok(q2, t, HALF))
                        last = score(bank[b][high, at_ + HALF:at_ + P], tok(k2, t, HALF, HALF),
                                     tok(q2, t, HALF, HALF))
                last.then_inc(unit_done, 1)

            READ = {X0: ((C0, 0, 0), (C1, 1, 0), (X0, 2, 0), (X1, 2, 256)),
                    X1: ((C0, 0, 128), (C1, 1, 128), (X0, 2, 128), (X1, 2, 384)),
                    C0: ((C0, 0, 256), (C1, 1, 256)),
                    C1: ((C0, 0, 384), (C1, 1, 384))}

            def head_outputs(h):
                pe.wait_ge(at_ok, h + 1)
                for t in range(NT):
                    if t == 3:
                        pe.wait_ge(o_out, h * 4 + 1)
                    for i, (kt, b, col) in enumerate(READ[t]):
                        last = pe.matmul(bank[4 + t % 3][:], at[:, b, col:col + P], v_sb[:, kt, :],
                                         start=(i == 0), stop=(i == len(READ[t]) - 1))
                    last.then_inc(o_ok, 1)

            def gla_head(h, before=None, gates=None):
                c = h * 3
                project(c, lambda t: c, False, ada=c, before=before)
                if gates is not None:
                    gates()
                gate_logits(h)
                project(c + 1, lambda t: c + 1, True, ada=c + 1,
                        after=lambda p: unit_scores(h, {2: 0, 6: 1}[p]) if p in (2, 6) else None)
                project(c + 2, lambda t: c + 2, True, ada=c + 2,
                        after=lambda p: unit_scores(h, {0: 2, 4: 3}[p]) if p in (0, 4) else None)
                head_outputs(h)

            pe.wait_ge(xn_ok, NT)
            gla_head(0, before=transposing(0, xn), gates=gate_columns)
            with pe.Fori(1, G_HEADS) as h:
                gla_head(h)

            def gate_rows(first, batches):
                for i in range(batches):
                    pe.wait_ge(diag_ok, first + i + 1)
                    pe.matmul(bank[5][:], ones[:], diag4.rearrange("p a b -> p (a b)"), start=True, stop=True)\
                        .then_inc(gate_t, 1)

            pe.wait_ge(u_ok, NT * G_HEADS)
            gate_rows(0, 8)
            pe.wait_ge(gate_ok, 8)
            project(OUT0, lambda t: OUT0, True, ada=OUT0, before=transposing(1, u))
            with pe.Fori(OUT0 + 1, DIFF) as c:
                project(c, lambda t: c, True, ada=c)

            def frees(h, second):
                def of(t):
                    return h * 2 + (DIFF + second) if t < 2 else h + DIFF
                return of

            def key_transposes(h):
                pe.wait_ge(k_ok, h + 1)
                for m in range(2):
                    for t in range(NT):
                        last = pe.transpose(bank[4 + m][:, t * P:(t + 1) * P], k_n[:, t, m * P:(m + 1) * P], ident[:])
                    last.then_inc(kt_t, 1)

            def query_transposes(h):
                pe.wait_ge(q_ok, h + 1)
                for m in range(2):
                    for t in range(2):
                        last = pe.transpose(bank[6][:, (2 * m + t) * P:(2 * m + t + 1) * P],
                                            q_t[:, t, m * P:(m + 1) * P], ident[:])
                last.then_inc(qt_t, 1)

            def attention_scores(h):
                pe.wait_ge(qT_ok, h + 1)
                pe.wait_ge(kT_ok, h * 2 + 2)
                for i in range(4):
                    t, m = i // 2, i % 2
                    pe.matmul(bank[4 + i][:], qT[:, m, t * P:(t + 1) * P], kT[:, m, :], start=True, stop=True)\
                        .then_inc(s_ok, 1)

            def weight_transposes(h):
                pe.wait_ge(a_ok, h * 2 + 2)
                for b in range(2):
                    for kt in (2 * b, 2 * b + 1):
                        for t in range(2):
                            at_ = (kt % 2) * 256 + t * P
                            last = pe.transpose(bank[4 + b][:, at_:at_ + P], probs[:, t, 0, kt * P:(kt + 1) * P], ident[:])
                    last.then_inc(at_t, 1)

            def attention_outputs(h):
                pe.wait_ge(aT_ok, h * 2 + 2)
                for t in range(2):
                    for kt in range(NT):
                        last = pe.matmul(bank[6][:, t * A_DV:(t + 1) * A_DV], aT[:, kt, t * P:(t + 1) * P],
                                         kv[:, kt, A_DV:CW], start=(kt == 0), stop=(kt == NT - 1))
                last.then_inc(pv_ok, 1)

            def attention_head(h, before=None, behind=None):
                c = h * 2 + DIFF
                project(c, frees(h, 0), True, before=before,
                        after=None if behind is None else lambda p: behind[p](h - 1) if p in behind else None)
                project(c + 1, frees(h, 1), True, tiles=2,
                        after=lambda p: key_transposes(h) if p == 5 else None)

            pe.wait_ge(xn_ok, 2 * NT)
            attention_head(0, before=transposing(2, xn))
            with pe.Fori(1, A_HEADS) as h:
                attention_head(h, behind={1: query_transposes, 2: attention_scores, 5: weight_transposes,
                                          6: attention_outputs})
            for step in (query_transposes, attention_scores, weight_transposes, attention_outputs):
                step(A_HEADS - 1)
            pe.wait_ge(u_ok, NT * G_HEADS + 2 * A_HEADS)
            gate_rows(8, 4)
            pe.wait_ge(gate_ok, 12)
            project(OUT1, lambda t: OUT1, True, tiles=2, before=transposing(3, u1, 2))
            with pe.Fori(OUT1 + 1, CHUNKS) as c:
                project(c, lambda t: c, True, tiles=2)

        @block.vector
        def _(dve):
            st = Steps(dve, dve_step)

            def complete(n, c, t, tiles=NT):
                if t == tiles - 1:
                    dve.wait_ge(pair_done, c * PAIRS + (PAIRS + RING))
                else:
                    dve.wait_ge(acc_ok, n + (t + 1))

            def newton(width):
                v, r, s = (stat[:, i, 0:width] for i in (1, 2, 3))
                st.step(dve.tensor_tensor(s, r, r, ALU.mult))
                st.wait()
                st.step(dve.tensor_tensor(s, s, v, ALU.mult))
                st.wait()
                st.step(dve.tensor_scalar(s, s, -0.5, 1.5, ALU.mult, ALU.add))
                st.wait()
                st.step(dve.tensor_tensor(r, r, s, ALU.mult))
                st.wait()

            def inverse_rms(n, width, count):
                dve.tensor_scalar(stat[:, 1, 0:width], stat[:, 0, 0:width], 1.0 / count, EPS, ALU.mult, ALU.add)\
                    .then_inc(mean_ok, 1)
                dve.wait_ge(rs_ok, n)
                newton(width)

            dve.wait_ge(cols_t, 1)
            dve.tensor_copy(cols1[:], bank[4][:, 0:V_ROWS]).then_inc(cols_ok, 1)
            dve.wait_ge(cols_t, 2)
            dve.tensor_copy(cols2[:], bank[5][:, 0:96]).then_inc(cols_ok, 1)
            dve.wait_ge(cols_ok, 2)
            lv = cols1[:, V_LAM:V_LAM + 4].rearrange("p (a b) -> p a b", b=2)
            dve.tensor_tensor(lam_pr, lv[:, :, 0], lv[:, :, 1], ALU.mult).then_inc(lam_pr_ok, 1)
            st.step(dve.tensor_scalar(cols1[:, V_SUB:V_SUB + 2], cols1[:, V_SUB:V_SUB + 2], 1.0 - LAMBDA_INIT,
                                      None, ALU.mult))
            dve.wait_ge(lam_e, 1)
            st.step(dve.tensor_tensor(lam[:, 2:3], lam[:, 0:1], lam[:, 1:2], ALU.subtract))
            st.wait()
            st.step(dve.tensor_scalar(lam[:, 3:4], lam[:, 2:3], LAMBDA_INIT, None, ALU.add))
            dve.wait_ge(a1_hi_ok, 1)
            dve.tensor_tensor(a1_lo[:], a1_raw, a1_hi[:].bitcast(F32), ALU.subtract).then_inc(a1_ok, 1)

            def row_norm(n):
                dve.wait_ge(sq_ok, NT if n == 1 else NT + NT * G_HEADS + NT)
                inverse_rms(n, NT, D)
                for t in range(NT):
                    dve.tensor_scalar(xn[:, t, :], u[:, t, :], stat[:, 2, t:t + 1], None, ALU.mult).then_inc(xn_ok, 1)

            row_norm(1)

            def take_modulation(s, tile0, c, startup=False, signal=True):
                if startup:
                    dve.wait_ge(ada0_used, c * PAIRS + PAIRS)
                else:
                    dve.wait_ge(ada_used, c * NK + (NK + 2))
                bias = cols2[:, bass.ds(tile0 + s * NK, 4)].unsqueeze(2).broadcast_to([P, 4, 2])
                taken = dve.tensor_tensor(mod[:, s, bass.ds(tile0, 4), :],
                                          bank[7][:, 0:8].rearrange("p (n m) -> p n m", m=2), bias, ALU.add)
                if signal:
                    taken.then_inc(ada_taken, 1)

            def scale_columns(layer, taken):
                dve.wait_ge(ada_taken, taken)
                s = mod[:, 3 * layer + 1]
                w = cols1[:, V_NORM + layer * NK:V_NORM + (layer + 1) * NK].unsqueeze(2).broadcast_to([P, NK, 2])
                st.step(dve.scalar_tensor_tensor(s, s, 1.0, w, ALU.add, ALU.mult))
                st.wait()

            with dve.Fori(0, 4) as a:
                take_modulation(0, a * 4, a, startup=True)
            with dve.Fori(0, 4) as a:
                take_modulation(1, a * 4, a + 4, startup=True)
            scale_columns(0, STARTUP)

            def modulated(layer):
                def emit(k, dst, src):
                    for m in range(2):
                        x = slice(m * 2 * P, (m + 1) * 2 * P)
                        last = dve.tensor_scalar(dst[:, x], src[:, x], mod[:, 3 * layer + 1, k, m:m + 1],
                                                 mod[:, 3 * layer, k, m:m + 1], ALU.mult, ALU.add)
                    return last
                return emit

            def weighted(col0, n, width):
                def emit(k, dst, src):
                    return dve.tensor_scalar(dst[:, 0:width], src[:, 0:width], cols1[:, col0 + k % n:col0 + k % n + 1],
                                             None, ALU.mult)
                return emit

            def activation_tiles(stage, buf, emit, width=TOK):
                def low(k):
                    dve.wait_ge(hi_ok, stage * NK + k + 1)
                    dve.tensor_tensor(lo[:, k, 0:width], buf[:, k % 2, 0:width], hi[:, k, 0:width].bitcast(F32),
                                      ALU.subtract).then_inc(acts_ok, 1)

                for k in range(NK):
                    dve.wait_ge(xt_ok, stage * NK + k + 1)
                    if k > 1:
                        dve.wait_ge(acts_ok, stage * NK + k - 1)
                    emit(k, buf[:, k % 2], bank[4 + k % 3]).then_inc(hf_ok, 1)
                    if k > 0:
                        low(k - 1)
                low(NK - 1)

            activation_tiles(0, hf, modulated(0))

            dve.wait_ge(const_in, CONSTS)

            def tokens(v, n):
                return v.rearrange("p (t s) -> p t s", s=n)

            def unit_tildes(h, n):
                back = n < 2
                b = bcum[:, n, :]
                b64, b128 = tokens(b, HALF), tokens(b, P)
                mid, split_at, tot = (HALF // 2, HALF, 0) if back else (HALF // 2 - 1, HALF - 1, P - 1)
                near, far = (slice(0, HALF), slice(HALF, P)) if back else (slice(HALF, P), slice(0, HALF))
                if n > 0:
                    dve.wait_ge(unit_done, h * 4 + n)
                dve.tensor_tensor(tokens(q2, HALF), b64, b64[:, :, mid:mid + 1].broadcast_to([P, 8, HALF]), ALU.subtract)
                dve.tensor_tensor(tokens(kb, P), b128, b128[:, :, tot:tot + 1].broadcast_to([P, NT, P]), ALU.subtract)
                ref = b128[:, :, split_at:split_at + 1].broadcast_to([P, NT, HALF])
                dve.tensor_tensor(q1, b128[:, :, near], ref, ALU.subtract)
                dve.tensor_tensor(k1, b128[:, :, far], ref, ALU.subtract).then_inc(d_ok, 1)
                q, k = qkT[:, n % 2, :], qkT[:, 2 + n % 2, :]
                dve.wait_ge(e_ok, h * 4 + (n + 1))
                st.step(dve.tensor_tensor(qh, qh, q, ALU.mult))
                dve.tensor_tensor(kb, kb, k, ALU.mult)
                dve.tensor_tensor(q2, q2, q, ALU.mult)
                dve.tensor_tensor(k2, k2, k, ALU.mult)
                dve.tensor_tensor(q1, q1, tokens(q, P)[:, :, near], ALU.mult)
                dve.tensor_tensor(k1, k1, tokens(k, P)[:, :, far], ALU.mult)
                st.wait()
                one, two, between = (X1, X0, C0) if back else (X0, X1, C1)
                dve.tensor_copy(qB[:, one * P:(one + 1) * P], qh[:, one * P:(one + 1) * P])
                st.step(dve.tensor_scalar(qB[:, two * P:(two + 1) * P], qh[:, two * P:(two + 1) * P],
                                          g_tot[:, one:one + 1], None, ALU.mult))
                st.wait()
                dve.tensor_scalar(qA, qB, g_tot[:, between:between + 1], None, ALU.mult).then_inc(til_ok, 1)

            DIAG = {X0: (2, 0), X1: (2, 384), C0: (0, 256), C1: (1, 384)}

            def gla_head(h, first):
                c = h * 3
                for t in range(NT):
                    complete(h * 9, c, t)
                    if t < 2:
                        dve.tensor_scalar(qkT[:, t], bank[t][:], G_DK ** -0.5, None, ALU.mult).then_inc(freed[t], 1)
                    else:
                        dve.tensor_copy(qkT[:, t], bank[t][:]).then_inc(freed[t], 1)
                take_modulation(2, h * 4, c)
                if first:
                    dve.wait_ge(z_ok, 1)
                    dve.tensor_copy(z_sb, bank[4][:, 0:TOK // 4].rearrange("p (t r) -> p t r", t=NT)).then_inc(z_sb_ok, 1)
                    for dr in range(2):
                        dve.wait_ge(zt_ok, dr + 1)
                        dve.tensor_copy(zT[32 * dr:32 * dr + G_RANK, :], bank[5 + dr][0:G_RANK, :]).then_inc(zT_ok, 1)
                else:
                    dve.wait_ge(u_ok, h * NT)
                for n in range(4):
                    dve.wait_ge(logit_ok, h * 4 + (n + 1))
                    dr = 1 if n < 2 else 0
                    bias = cols1[:, bass.ds(h * 2 + (V_GATEB + 8 * dr + n % 2), 1)]
                    dve.tensor_scalar(bcum[:, n], bank[4 + n % 3][:], bias, None, ALU.add).then_inc(logit_out, 1)
                dve.wait_ge(ln_ok, h + 1)
                st.step(dve.scalar_tensor_tensor(ln_t.rearrange("p a b -> p (a b)"), bcum.rearrange("p a b -> p (a b)"),
                                                 0.0, ln_t.rearrange("p a b -> p (a b)"), ALU.min, ALU.subtract))
                st.wait()
                for n in range(4):
                    for t in range(NT):
                        src, dst = ln_t[:, n, t * P:(t + 1) * P], bcum[:, n, t * P:(t + 1) * P]
                        if n < 2:
                            src, dst = src[:, ::-1], dst[:, ::-1]
                        last = dve.tensor_tensor_scan(dst, ones[:], src, 0.0, ALU.mult, ALU.add)
                st.step(last)
                st.wait()
                unit_tildes(h, 0)
                unit_tildes(h, 1)
                for t in range(NT):
                    complete(h * 9 + 3, c + 1, t)
                    dve.tensor_copy(v_sb[:, t], bank[t][:]).then_inc(freed[t], 1)
                dve.wait_ge(unit_done, h * 4 + 2)
                take_modulation(3, h * 4, c + 1, signal=False)
                d2 = bank[7][:, 256:512].rearrange("p (t s) -> p t s", s=HALF)
                for half in range(2):
                    r = slice(half * HALF, (half + 1) * HALF)
                    last = dve.copy_predicated(d2m[r, :, r], mask2[r].unsqueeze(1).broadcast_to([HALF, NT, HALF]), d2[r])
                last.then_inc(ada_taken, 1)
                unit_tildes(h, 2)
                unit_tildes(h, 3)
                dve.wait_ge(unit_done, h * 4 + 4)
                dve.tensor_copy(at[:, 0, 0:256], bank[4][:, 0:256])
                for t in range(NT):
                    b, col = DIAG[t]
                    last = dve.copy_predicated(d1m[:, t, :], mask1[:], bank[4 + b][:, col:col + P])
                st.step(last)
                dve.tensor_copy(at[:, 0, 384:512], bank[4][:, 384:512])
                dve.tensor_copy(at[:, 1, 0:384], bank[5][:, 0:384])
                dve.tensor_copy(at[:, 2, 128:384], bank[6][:, 128:384])
                st.wait()
                for t in range(NT):
                    b, col = DIAG[t]
                    last = dve.tensor_tensor(at[:, b, col:col + P], d1m[:, t, :], d2m[:, t, :], ALU.add)
                last.then_inc(at_ok, 1)
                take_modulation(4, h * 4, c + 2)
                for t in range(NT):
                    dve.wait_ge(o_ok, h * 4 + (t + 1))
                    dve.tensor_copy(o_sb[:, t], bank[4 + t % 3][:]).then_inc(o_out, 1)
                dve.wait_ge(sq_ok, h * NT + 2 * NT)
                inverse_rms(h + 2, NT, G_DV)
                for t in range(NT):
                    dve.scalar_tensor_tensor(u[:, t, bass.ds(h * G_DV, G_DV)], o_sb[:, t], stat[:, 2, t:t + 1],
                                             silu_g[:, t], ALU.mult, ALU.mult).then_inc(u_ok, 1)

            n0 = st.n
            gla_head(0, True)
            per = st.n - n0
            with dve.Fori(1, G_HEADS) as h:
                st.enter(h - 1, per)
                gla_head(h, False)
                st.leave(G_HEADS - 1)

            def gate_rows(s, cond, batch0):
                for i in range(4):
                    n = batch0 + i
                    if n > 0:
                        dve.wait_ge(gate_t, n)
                    dve.tensor_tensor(diag4, ident[:].unsqueeze(1).broadcast_to([P, 4, P]),
                                      mod[:, s, 4 * i:4 * i + 4, cond:cond + 1].broadcast_to([P, 4, P]), ALU.mult)\
                        .then_inc(diag_ok, 1)
                    dve.wait_ge(gate_t, n + 1)
                    dve.tensor_copy(gate_row[:, cond, i * CW:(i + 1) * CW], bank[5][:]).then_inc(gate_ok, 1)

            dve.wait_ge(u_ok, NT * G_HEADS)
            dve.wait_ge(ada_taken, STARTUP + OUT0)
            gate_rows(2, 0, 0)
            gate_rows(2, 1, 4)
            activation_tiles(1, hfu, weighted(V_GN, G_DV // P, TOK))

            with dve.Fori(0, 4) as j:
                c = j + OUT0
                dve.wait_ge(xres_in, j * 64 + 64)
                for t in range(NT):
                    complete(j * 3 + 3 * OUT0, c, t)
                    dve.tensor_tensor(yrow[:, t], bank[t][:], gate_row[:, t // 2, bass.ds(j * CW, CW)], ALU.mult)\
                        .then_inc(freed[t], 1)
                    dve.wait_ge(freed[t], c + 1)
                    dve.tensor_tensor(u[:, t, bass.ds(j * CW, CW)], yrow[:, t], xres[:, t], ALU.add).then_inc(x1_ok, 1)
                take_modulation(5, j * 4, c)

            row_norm(G_HEADS + 2)
            scale_columns(1, STARTUP + DIFF)
            activation_tiles(2, hf, modulated(1))

            dve.wait_ge(rows_in, 16 * 6)

            def swapped(dst, src, tab):
                def g(v):
                    return v.rearrange("p t (g a s) -> p t g a s", a=2, s=32)
                for a in range(2):
                    last = dve.tensor_tensor(g(dst)[:, :, :, a], g(src)[:, :, :, 1 - a], g(tab)[:, :, :, a], ALU.mult)
                return last

            for i, w in ((0, silu_ag[:, 0]), (2, knw)):
                for t in range(2):
                    dve.tensor_tensor(rope[:, i, t], rope[:, i, t], w, ALU.mult)
                    last = swapped(rope[:, i + 1, t:t + 1], w.unsqueeze(1), rope[:, i + 1, t:t + 1])
            last.then_inc(rope_ok, 1)
            dve.wait_ge(rope_ok, 1)

            def flat(v):
                return v.rearrange("p a b -> p (a b)")

            def rotate(n, tmp, i, normed_into):
                a, b = tmp
                dve.tensor_tensor(a, n, rope[:, i], ALU.mult)
                st.step(swapped(b, n, rope[:, i + 1]))
                st.wait()
                return dve.tensor_tensor(normed_into, a, b, ALU.add)

            def squares(dst, src, groups):
                st.step(dve.tensor_tensor(dst, src, src, ALU.mult))
                st.wait()
                st.step(dve.tensor_reduce(stat[:, 0, 0:groups],
                                          flat(dst).rearrange("p (g d) -> p g d", g=groups), AX.X, ALU.add))
                st.wait()

            BATCH = G_HEADS + 2

            def keys(h):
                c = h * 2 + DIFF
                for t in range(NT):
                    complete(h * 4 + 3 * DIFF, c, t)
                    dve.tensor_copy(kv[:, t], bank[t][:]).then_inc(freed[t], 1)
                dve.wait_ge(freed[3], h + DIFF + 1)
                k_raw = kv[:, :, 0:256]
                squares(k_t, k_raw, 8)
                inverse_rms(h * 3 + (BATCH + 1), 8, A_D)
                rs = stat[:, 2, 0:8].rearrange("p (t m) -> p t m", m=2)
                for m in range(2):
                    last = dve.tensor_tensor(k_n[:, :, m * P:(m + 1) * P], k_raw[:, :, m * P:(m + 1) * P],
                                             rs[:, :, m:m + 1].broadcast_to([P, NT, P]), ALU.mult)
                st.step(last)
                st.wait()
                dve.tensor_tensor(k_n[:, 2:4], k_n[:, 2:4], knw.unsqueeze(1).broadcast_to([P, 2, 256]), ALU.mult)
                rotate(k_n[:, 0:2], (k_t[:, 0:2], k_t[:, 2:4]), 2, k_n[:, 0:2]).then_inc(k_ok, 1)
                for m in range(2):
                    dve.wait_ge(kt_t, h * 2 + (m + 1))
                    dve.tensor_copy(kT[:, m], bank[4 + m][:]).then_inc(kT_ok, 1)

            def queries(h):
                c = h * 2 + (DIFF + 1)
                for t in range(2):
                    complete(h * 4 + (3 * DIFF + 3), c, t, 2)
                    dve.tensor_copy(qg[:, t], bank[t][:]).then_inc(freed[t], 1)
                dve.wait_ge(freed[1], h * 2 + (DIFF + 2))
                q_raw = qg[:, :, 0:256]
                squares(q_t, q_raw, 4)
                inverse_rms(h * 3 + (BATCH + 2), 4, A_D)
                rs = stat[:, 2, 0:4].rearrange("p (t m) -> p t m", m=2)
                for m in range(2):
                    last = dve.tensor_tensor(q_raw[:, :, m * P:(m + 1) * P], q_raw[:, :, m * P:(m + 1) * P],
                                             rs[:, :, m:m + 1].broadcast_to([P, 2, P]), ALU.mult)
                st.step(last)
                st.wait()
                rotate(q_raw, (q_t, q_u), 0, q_t).then_inc(q_ok, 1)

            def attend(h):
                dve.wait_ge(qt_t, h + 1)
                dve.tensor_copy(qT.rearrange("p m n -> p (m n)"), bank[6][:]).then_inc(qT_ok, 1)
                for i in range(4):
                    dve.wait_ge(s_ok, h * 4 + (i + 1))
                    st.step(dve.tensor_reduce(smx[:, 3, i:i + 1], bank[4 + i][:], AX.X, ALU.max))
                    st.wait()
                    dve.tensor_scalar(smx[:, 0, i:i + 1], smx[:, 3, i:i + 1], -(A_D ** -0.5), None, ALU.mult)\
                        .then_inc(max_ok, 1)
                for t in range(2):
                    s0, s1 = smx[:, 2, 2 * t:2 * t + 1], smx[:, 2, 2 * t + 1:2 * t + 2]
                    dve.wait_ge(p_ok, h * 4 + (2 * t + 2))
                    st.step(dve.reciprocal(smx[:, 2, 2 * t:2 * t + 2], smx[:, 1, 2 * t:2 * t + 2]))
                    st.wait()
                    st.step(dve.tensor_tensor(s1, s1, lam[:, 3:4], ALU.mult))
                    st.wait()
                    st.step(dve.tensor_scalar(probs[:, t, 1], probs[:, t, 1], s1, None, ALU.mult))
                    st.wait()
                    dve.scalar_tensor_tensor(probs[:, t, 0], probs[:, t, 0], s0, probs[:, t, 1], ALU.mult,
                                             ALU.subtract).then_inc(a_ok, 1)
                for b in range(2):
                    dve.wait_ge(at_t, h * 2 + (b + 1))
                    dve.tensor_copy(flat(aT[:, 2 * b:2 * b + 2]), bank[4 + b][:]).then_inc(aT_ok, 1)
                dve.wait_ge(pv_ok, h + 1)
                st.step(dve.tensor_copy(flat(o1), bank[6][:]))
                st.wait()
                squares(q_u, o1, 2)
                inverse_rms(h * 3 + (BATCH + 3), 2, A_DV)
                dve.wait_ge(g_ok, h + 1)
                for t in range(2):
                    dve.scalar_tensor_tensor(u1[:, t, bass.ds(h * A_DV, A_DV)], o1[:, t], stat[:, 2, t:t + 1],
                                             silu_ag[:, t], ALU.mult, ALU.mult).then_inc(u_ok, 1)

            keys(0)
            queries(0)
            with dve.Fori(1, A_HEADS) as h:
                st.enter(h - 1, 33)
                attend(h - 1)
                keys(h)
                queries(h)
                st.leave(A_HEADS - 1)
            attend(A_HEADS - 1)

            dve.wait_ge(u_ok, NT * G_HEADS + 2 * A_HEADS)
            gate_rows(5, 0, 8)
            activation_tiles(3, hfu, weighted(V_SUB, A_DV // P, 2 * P), 2 * P)
            def result(j, first):
                if not first:
                    dve.wait_ge(y_out, j * 32)
                for t in range(2):
                    complete(j + (3 * DIFF + 4 * A_HEADS), j + OUT1, t, 2)
                    dve.tensor_tensor(yrow[:, t], bank[t][:], gate_row[:, 0, bass.ds(j * CW, CW)], ALU.mult)\
                        .then_inc(freed[t], 1)
                    dve.wait_ge(freed[t], j + (OUT1 + 1))
                    dve.tensor_tensor(yrow[:, t], yrow[:, t], u[:, t, bass.ds(j * CW, CW)], ALU.add)\
                        .then_inc(y_ok, 1)

            result(0, True)
            with dve.Fori(1, 4) as j:
                result(j, False)


INPUTS = ("x", "c", "ctx", "c_ctx", "norm_w", "ada_w", "ada_b", "gla_w_in", "gla_gate_a1", "gla_gate_a2",
          "gla_gate_b", "gla_gn_w", "gla_w_out", "diff_w_in", "diff_qn_w", "diff_kn_w", "diff_lam",
          "diff_subln_w", "diff_w_out")


def constants():
    n = 2 * P
    row = np.repeat(np.arange(n // GRID_W), GRID_W).astype(np.float32)
    col = np.tile(np.arange(GRID_W), n // GRID_W).astype(np.float32)
    half = A_D // 2
    freq = (np.float32(ROPE_BASE) ** (-np.arange(0, half, 2, dtype=np.float32) / np.float32(half))).astype(np.float32)
    ang = np.concatenate([row[:, None] * freq] * 2 + [col[:, None] * freq] * 2, axis=1)
    sign = np.tile(np.repeat(np.float32([-1, 1]), A_D // 4), 2)
    j, i = np.arange(P)[:, None], np.arange(P)[None, :]
    return {
        "cos": np.tile(np.cos(ang), (1, 2)).astype(np.float32),
        "sin": np.tile(np.sin(ang) * sign, (1, 2)).astype(np.float32),
        "ident": np.eye(P, dtype=np.float32),
        "mask1": ((j <= i) | ((j >= HALF) & (i < HALF))).astype(np.int32),
        "mask2": ((j % HALF) >= np.arange(HALF)[None, :]).astype(np.int32),
    }


def kernel(**inputs):
    import concourse.bacc as bacc
    from concourse.bass_utils import run_bass_kernel_spmd

    nc = bacc.Bacc("TRN2", target_bir_lowering=False, num_devices=1)
    arrays, io = {}, {}
    for name, a in list((n, inputs[n]) for n in INPUTS) + list(constants().items()):
        a = np.ascontiguousarray(a)
        arrays[f"in_{name}"] = a
        io[name] = nc.dram_tensor(f"in_{name}", a.shape, mybir.dt.from_np(a.dtype), kind="ExternalInput").ap()
    out = nc.dram_tensor("result", (1, 2 * P, D), F32, kind="ExternalOutput").ap()
    build(nc, io, out)
    return run_bass_kernel_spmd(nc, [arrays], core_ids=[0]).results[0]["result"]
```

```python
import math
from contextlib import ExitStack

import numpy as np

import concourse.bass as bass
from concourse import mybir

F32 = mybir.dt.float32
F32R = mybir.dt.float32r
I32 = mybir.dt.int32
ACT = mybir.ActivationFunctionType
ALU = mybir.AluOpType
AX = mybir.AxisListType

P = 128
D = 2048
NT = 4
TOK = NT * P
X0, X1, C0, C1 = range(NT)
NK = D // P
CW = 512
PAIRS = NK // 2
RING = 4
EPS = 1e-6
GRID_W = 64
ROPE_BASE = 10000.0

G_HEADS, G_DK, G_DV, G_RANK = 4, 256, 512, 16
G_NORM = 16.0
HALF = 64
A_HEADS, A_D, A_DV = 8, 128, 256
LAMBDA_INIT = 0.8 - 0.6 * math.exp(-0.3)

OUT0 = 3 * G_HEADS
DIFF = OUT0 + 4
OUT1 = DIFF + 2 * A_HEADS
CHUNKS = OUT1 + 4
STARTUP = 8

V_C, V_CCTX, V_NORM, V_GATEB, V_GN, V_LAM, V_SUB, V_ROWS = 0, 16, 32, 64, 80, 84, 88, 90


class Steps:

    def __init__(self, eng, sem):
        self.eng, self.sem, self.base, self.n = eng, sem, 0, 0

    def step(self, ins):
        ins.then_inc(self.sem, 1)
        self.n += 1

    def wait(self):
        self.eng.wait_ge(self.sem, self.base + self.n)

    def enter(self, i, per):
        self.start, self.per = self.base + self.n, per
        self.base, self.n = i * per + self.start, 0

    def leave(self, rounds):
        assert self.n == self.per, f"{self.n} steps in a round, not {self.per}"
        self.base, self.n = self.start + rounds * self.per, 0


def build(nc, io, out):
    with ExitStack() as ctx:
        def sb(name, shape, dt=F32):
            return ctx.enter_context(nc.sbuf_tensor(name, shape, dt))

        def sem(name):
            return ctx.enter_context(nc.semaphore(name))

        hi = sb("acts_hi", [P, NK, TOK], F32R)
        lo = sb("acts_lo", [P, NK, TOK], F32R)
        w_hi = sb("w_hi", [P, RING, 2, CW], F32R)
        w_lo = sb("w_lo", [P, RING, 2, CW], F32R)
        a1 = sb("a1", [P, NK, 2, 2 * G_RANK], F32R)
        raw = sb("w_raw", [P, RING, 2, CW])
        ada_w = sb("ada_w", [P, 2, CW])
        u = sb("u", [P, NT, D])
        work = sb("work", [P, 10752])
        ident = sb("ident_sb", [P, P])
        ones = sb("ones", [P, P])
        mask1 = sb("mask1_sb", [P, P], I32)
        mask2 = sb("mask2_sb", [P, HALF], I32)
        zT = sb("gate_zT", [48, TOK])
        a2 = sb("gate_a2", [48, G_DK])
        cols1 = sb("cols1", [P, V_ROWS])
        cols2 = sb("cols2", [P, 96])
        silu_c = sb("silu_c", [P, NK, 2])
        mod = sb("mod", [P, 6, NK, 2])
        d1m = sb("d1m", [P, NT, P])
        d2m = sb("d2m", [P, NT, P])
        g_tot = sb("g_tot", [P, NT])
        stat = sb("stat", [P, 4, 8])
        smx = sb("softmax_stat", [P, 4, 4])
        lam = sb("lam", [P, 8])

        def view(at, *shape):
            n = int(np.prod(shape))
            v = work[:, at:at + n]
            if len(shape) == 1:
                return v
            names = "abcd"[:len(shape)]
            kw = {names[i]: shape[i] for i in range(1, len(shape))}
            return v.rearrange(f"p ({' '.join(names)}) -> p {' '.join(names)}", **kw)

        xn = view(0, NT, D)
        hf = view(NT * D, 2, TOK)
        a1_raw = view(NT * D + 2 * TOK, NK, 2 * G_RANK)
        mod_acc = view(9728, 2, CW)
        startup_acc = [mod_acc, hf]
        mod_acc_g = u[:, 2:4, D - CW:D]
        mod_acc_v = u[:, 0:2, D - CW:D]
        vec1 = view(9728, P)
        vec2 = view(9856, P)
        lam_pr = view(9984, 2)
        qkT = view(0, 4, TOK)
        v_sb = view(2048, NT, CW)
        bcum = view(4096, 4, TOK)
        silu_g = view(4096, NT, CW)
        t0 = 6144
        ln_t = view(t0, 4, TOK)
        qh = view(t0, TOK)
        kb = view(t0 + 512, TOK)
        q2 = view(t0 + 1024, TOK)
        k2 = view(t0 + 1536, TOK)
        q1 = view(t0 + 2048, NT, HALF)
        k1 = view(t0 + 2304, NT, HALF)
        qA = view(t0 + 2560, 2 * P)
        qB = view(t0 + 2816, 2 * P)
        o_sb = view(t0, NT, CW)
        o_sq = view(t0 + 2048, CW)
        z_sb = view(t0 + 2560, NT, 2 * G_RANK)
        at = view(t0 + 3072, 3, CW)
        gate_row = view(0, 2, D)
        xres = view(4096, NT, CW)
        yrow = view(6144, NT, CW)
        diag4 = [view(8192, 4, P), view(8704, 4, P)]
        hfu = view(8704, 2, TOK)
        rope = view(0, 4, 2, 256)
        knw = view(2048, 256)
        silu_ag = view(2304, 2, A_DV)
        kv = view(2816, NT, CW)
        qg = view(4864, 2, CW)
        kT = view(5888, 2, TOK)
        qT = view(6912, 2, 2 * P)
        probs = view(7424, 2, 2, CW)
        k_n = view(7424, NT, 256)
        k_t = view(8448, NT, 256)
        aT = view(9472, NT, 2 * P)
        q_t = view(9472, 2, 256)
        q_u = view(9984, 2, 256)
        o1 = q_t
        u1 = u[:, 2:4, :]

        bank = [ctx.enter_context(nc.psum_tensor(f"bank{i}", [P, CW], F32)) for i in range(8)]

        vec_in, const_in, x_in, a1_in, a2_in = (sem(n) for n in ("vec_in", "const_in", "x_in", "a1_in", "a2_in"))
        raw_in = [sem(f"raw_in{i}") for i in range(RING)]
        ada_in = [sem(f"ada_in{i}") for i in range(2)]
        xres_in = sem("xres_in")
        rows_in = sem("rows_in")
        rope_ok = sem("rope_ok")
        cols_t = sem("cols_t")
        cols_ok = sem("cols_ok")
        silu_ok = sem("silu_ok")
        ada0_pe = sem("ada0_pe")
        ada0_dve = sem("ada0_dve")
        ada_used = sem("ada_used")
        mod_sum = sem("mod_sum")
        d2_ok = sem("d2_ok")
        ada_taken = sem("ada_taken")
        w_hi_ok = sem("w_hi_ok")
        w_split = sem("w_split")
        pair_done = sem("pair_done")
        acc_ok = sem("acc_ok")
        freed = [sem(f"freed{i}") for i in range(NT)]
        sq_ok = sem("sq_ok")
        mean_ok = sem("mean_ok")
        rs_ok = sem("rs_ok")
        xn_ok = sem("xn_ok")
        xt_ok = sem("xt_ok")
        hf_ok = sem("hf_ok")
        hi_ok = sem("hi_ok")
        acts_ok = sem("acts_ok")
        a1_hi_ok, a1_ok, z_ok, z_sb_ok, zt_ok, zT_ok = (
            sem(n) for n in ("a1_hi_ok", "a1_ok", "z_ok", "z_sb_ok", "zt_ok", "zT_ok"))
        logit_ok = sem("logit_ok")
        logit_out = sem("logit_out")
        ln_ok = sem("ln_ok")
        d_ok = sem("d_ok")
        e_ok = sem("e_ok")
        til_ok = sem("til_ok")
        unit_done = sem("unit_done")
        at_ok = sem("at_ok")
        o_ok = sem("o_ok")
        o_out = sem("o_out")
        g_ok = sem("g_ok")
        u_ok = sem("u_ok")
        diag_ok, gate_t, gate_ok = sem("diag_ok"), sem("gate_t"), sem("gate_ok")
        x1_ok = sem("x1_ok")
        k_ok = sem("k_ok")
        kt_t = sem("kt_t")
        kT_ok = sem("kT_ok")
        q_ok = sem("q_ok")
        qt_t = sem("qt_t")
        qT_ok = sem("qT_ok")
        s_ok = sem("s_ok")
        max_ok = sem("max_ok")
        p_ok = sem("p_ok")
        a_ok = sem("a_ok")
        at_t = sem("at_t")
        aT_ok = sem("aT_ok")
        pv_ok = sem("pv_ok")
        lam_t, lam_pr_ok, lam_e, lam_ok = sem("lam_t"), sem("lam_pr_ok"), sem("lam_e"), sem("lam_ok")
        y_ok = sem("y_ok")
        y_out = sem("y_out")
        dve_step = sem("dve_step")
        act_step = sem("act_step")

        block = ctx.enter_context(nc.Block())

        @block.sync
        def _(sp):
            for dst, src in (
                (vec1[V_C:V_C + NK], io["c"].rearrange("o (k p) -> (o k) p", p=P)),
                (vec1[V_CCTX:V_CCTX + NK], io["c_ctx"].rearrange("(k p) -> k p", p=P)),
                (vec1[V_NORM:V_NORM + 2 * NK], io["norm_w"].rearrange("l (k p) -> (l k) p", p=P)),
                (vec1[V_GATEB:V_GATEB + 16], io["gla_gate_b"].rearrange("o d (k p) -> (o d k) p", p=P)),
                (vec1[V_GN:V_GN + 4], io["gla_gn_w"].rearrange("o (k p) -> (o k) p", p=P)),
                (vec1[V_LAM:V_LAM + 4], io["diff_lam"].rearrange("o r p -> (o r) p")),
                (vec1[V_SUB:V_SUB + 2], io["diff_subln_w"].rearrange("o (k p) -> (o k) p", p=P)),
                (vec2[0:96], io["ada_b"].rearrange("l (k p) -> (l k) p", p=P)),
            ):
                sp.dma_start(dst, src).then_inc(vec_in, 16)
            for dst, src in ((ident[:], io["ident"]), (mask1[:], io["mask1"]), (mask2[:], io["mask2"])):
                sp.dma_start(dst, src).then_inc(const_in, 16)
            sp.sem_inc(w_split, RING)
            sp.sem_inc(pair_done, RING)
            sp.sem_inc(ada_used, 2)

            aw0 = io["ada_w"][0].rearrange("(k p) n -> p k n", p=P)
            aw1 = io["ada_w"][1].rearrange("(k p) n -> p k n", p=P)

            def startup_chunk(a, first):
                for p in range(PAIRS):
                    if not (first and p < RING):
                        sp.wait_ge(ada0_pe, a * PAIRS + (p - RING + 1))
                        sp.wait_ge(ada0_dve, a * PAIRS + (p - RING + 1))
                    sp.dma_start(raw[:, p % RING], aw0[:, 2 * p:2 * p + 2, bass.ds(a * CW, CW)])\
                        .then_inc(raw_in[p % RING], 16)

            startup_chunk(0, True)
            for t in range(NT):
                src = io["x"][0] if t < C0 else io["ctx"][0]
                sp.dma_start(u[:, t, :], src[(t % 2) * P:(t % 2 + 1) * P, :]).then_inc(x_in, 16)
            for dr in range(2):
                sp.dma_start(a1_raw[:, :, dr * G_RANK:(dr + 1) * G_RANK],
                             io["gla_gate_a1"][0, dr].rearrange("(k p) r -> p k r", p=P)).then_inc(a1_in, 16)
            with sp.Fori(1, STARTUP) as a:
                startup_chunk(a, False)
            sp.wait_ge(ada0_pe, STARTUP * PAIRS)
            sp.wait_ge(ada0_dve, STARTUP * PAIRS)

            def load_pair(c, p, parts):
                moves = parts(p)
                sp.wait_ge(w_split, c * PAIRS + (p + 1))
                for dst, src in moves:
                    sp.dma_start(dst, src).then_inc(raw_in[p % RING], 16)

            def side_by_side(w, first, second):
                n = CW // 2

                def parts(p):
                    slot = raw[:, p % RING]
                    return [(slot[:, :, n:CW], w[:, 2 * p:2 * p + 2, bass.ds(second, n)]),
                            (slot[:, :, 0:n], w[:, 2 * p:2 * p + 2, bass.ds(first, n)])]
                return parts

            def one_range(w, first):
                def parts(p):
                    return [(raw[:, p % RING, j], w[:, 2 * p + j, bass.ds(first, CW)]) for j in range(2)]
                return parts

            def load_chunk(c, parts, following, ada_from=None):
                for p in range(PAIRS):
                    if p < RING:
                        load_pair(c, p + RING, parts)
                    elif following is not None:
                        load_pair(c + 1, p - RING, following)
                    if ada_from is not None:
                        for k in (2 * p, 2 * p + 1):
                            sp.wait_ge(ada_used, c * NK + (k + 1))
                            sp.dma_start(ada_w[:, k % 2], ada_from[0][:, k, bass.ds(ada_from[1], CW)])\
                                .then_inc(ada_in[k % 2], 16)

            wg = io["gla_w_in"][0].rearrange("(k p) n -> p k n", p=P)
            wo = io["gla_w_out"][0].rearrange("(k p) n -> p k n", p=P)
            wd = io["diff_w_in"][0].rearrange("(k p) n -> p k n", p=P)
            w1 = io["diff_w_out"][0].rearrange("(k p) n -> p k n", p=P)
            key0, val0, gate0 = 1024, 2048, 4096

            def q_and_k(h):
                return side_by_side(wg, h * G_DK, h * G_DK + key0)

            def gla_head(h, following):
                if not (isinstance(h, int) and h == 0):
                    sp.wait_ge(logit_ok, h * 4)
                for dr in range(2):
                    sp.dma_start(a2[32 * dr:32 * dr + G_RANK, :],
                                 io["gla_gate_a2"][0, dr][:, bass.ds(h * G_DK, G_DK)]).then_inc(a2_in, 16)
                c = h * 3
                v, g = one_range(wg, h * G_DV + val0), one_range(wg, h * G_DV + gate0)
                load_chunk(c, q_and_k(h), v, (aw0, h * CW + 2 * D))
                load_chunk(c + 1, v, g, (aw1, h * CW))
                load_chunk(c + 2, g, following, (aw1, h * CW + D))

            def out0(j, following):
                load_chunk(j + OUT0, one_range(wo, j * CW), following, (aw1, j * CW + 2 * D))

            def k_and_v(h):
                return side_by_side(wd, h * A_DV + D, h * A_DV + 2 * D)

            def attention_head(h, following):
                c = h * 2 + DIFF
                q_and_g = side_by_side(wd, h * A_DV, h * A_DV + 3 * D)
                load_chunk(c, k_and_v(h), q_and_g)
                load_chunk(c + 1, q_and_g, following)

            for p in range(RING):
                load_pair(0, p, q_and_k(0))
            gla_head(0, q_and_k(1))
            with sp.Fori(1, G_HEADS - 1) as h:
                gla_head(h, q_and_k(h + 1))
            gla_head(G_HEADS - 1, one_range(wo, 0))
            with sp.Fori(0, 3) as j:
                out0(j, one_range(wo, (j + 1) * CW))
            out0(3, k_and_v(0))
            with sp.Fori(0, A_HEADS - 1) as h:
                attention_head(h, k_and_v(h + 1))
            attention_head(A_HEADS - 1, one_range(w1, 0))
            with sp.Fori(0, 3) as j:
                load_chunk(j + OUT1, one_range(w1, j * CW), one_range(w1, (j + 1) * CW))
            load_chunk(CHUNKS - 1, one_range(w1, 3 * CW), None)

        @block.gpsimd
        def _(pool):
            pool.memset(ones[:], 1.0).then_inc(const_in, 1)
            pool.memset(d1m[:], 0.0).then_inc(const_in, 1)
            pool.memset(d2m[:], 0.0).then_inc(const_in, 1)
            with pool.Fori(0, CHUNKS) as c:
                for p in range(PAIRS):
                    pool.wait_ge(w_hi_ok, c * PAIRS + (p + 1))
                    pool.tensor_tensor(w_lo[:, p % RING], raw[:, p % RING], w_hi[:, p % RING].bitcast(F32),
                                       ALU.subtract).then_inc(w_split, 1)

        CONSTS = 3 * 16 + 3

        @block.scalar
        def _(act):
            st = Steps(act, act_step)

            def split(c, p):
                act.wait_ge(raw_in[p % RING], c * 64 + (16 * 2 * STARTUP + 32 * (p // RING + 1)))
                act.wait_ge(pair_done, c * PAIRS + (p + 1))
                act.activation(w_hi[:, p % RING], raw[:, p % RING], ACT.Copy).then_inc(w_hi_ok, 1)

            def splits(c, ps):
                for p in ps:
                    split(c, p)

            def rsqrt(n, width):
                act.wait_ge(mean_ok, n)
                st.step(act.activation(stat[:, 3, 0:width], stat[:, 1, 0:width], ACT.Ln))
                st.wait()
                act.activation(stat[:, 2, 0:width], stat[:, 3, 0:width], ACT.Exp, scale=-0.5).then_inc(rs_ok, 1)

            def row_squares():
                for t in range(NT):
                    act.activation(xn[:, t, :], u[:, t, :], ACT.Square, accum_out=stat[:, 0, t:t + 1])\
                        .then_inc(sq_ok, 1)

            def high_parts(stage, src, c):
                n = NT if stage < 3 else 2
                for k in range(NK):
                    if k >= 4 and k % 2 == 0 and k < 12:
                        split(c, k // 2 + 2)
                    act.wait_ge(hf_ok, stage * NK + k + 1)
                    act.activation(hi[:, k, 0:n * P], src[:, k % 2, 0:n * P], ACT.Copy).then_inc(hi_ok, 1)

            act.wait_ge(cols_ok, 1)
            for m in range(2):
                act.activation(silu_c[:, :, m], cols1[:, m * NK:(m + 1) * NK], ACT.Silu).then_inc(silu_ok, 1)
            act.wait_ge(lam_t, 1)
            act.activation(lam[:, 0:2], bank[4][:, 0:2], ACT.Exp).then_inc(lam_e, 1)
            act.wait_ge(a1_in, 32)
            act.activation(a1[:, :, 0], a1_raw, ACT.Copy).then_inc(a1_hi_ok, 1)
            act.wait_ge(x_in, 16 * NT)
            row_squares()
            rsqrt(1, NT)
            splits(0, range(4))
            high_parts(0, hf, 0)

            def decays(h, n):
                b = bcum[:, n, :]
                act.wait_ge(d_ok, h * 4 + (n + 1))
                st.step(act.activation(k2, q2, ACT.Exp, scale=-1.0 / G_NORM))
                act.activation(qh, b, ACT.Exp, scale=1.0 / G_NORM)
                act.activation(kb, kb, ACT.Exp, scale=-1.0 / G_NORM)
                act.activation(q1, q1, ACT.Exp, scale=1.0 / G_NORM)
                act.activation(k1, k1, ACT.Exp, scale=-1.0 / G_NORM)
                last = 0 if n < 2 else P - 1
                act.activation(g_tot[:], b.rearrange("p (t s) -> p t s", s=P)[:, :, last], ACT.Exp,
                               scale=1.0 / G_NORM)
                st.wait()
                act.activation(q2, q2, ACT.Exp, scale=1.0 / G_NORM).then_inc(e_ok, 1)

            def gla_head(h, first):
                c = h * 3
                if not first:
                    splits(c, range(4, 8))
                splits(c + 1, range(0, 4))
                for n in range(4):
                    act.wait_ge(logit_out, h * 4 + (n + 1))
                    st.step(act.activation(ln_t[:, n], bcum[:, n], ACT.Abs))
                    st.wait()
                    st.step(act.activation(ln_t[:, n], ln_t[:, n], ACT.Exp, scale=-1.0))
                    st.wait()
                    act.activation(ln_t[:, n], ln_t[:, n], ACT.Ln, bias=1.0).then_inc(ln_ok, 1)
                splits(c + 1, range(4, 5))
                decays(h, 0)
                splits(c + 1, range(5, 8))
                splits(c + 2, range(0, 2))
                decays(h, 1)
                splits(c + 2, range(2, 5))
                decays(h, 2)
                splits(c + 2, range(5, 8))
                decays(h, 3)
                splits(c + 3, range(0, 4))
                for t in range(NT):
                    if t == NT - 1:
                        act.wait_ge(pair_done, c * PAIRS + (3 * PAIRS + RING))
                    else:
                        act.wait_ge(acc_ok, c * 3 + (6 + t + 1))
                    act.activation(silu_g[:, t], bank[t][:], ACT.Silu).then_inc(freed[t], 1)
                for t in range(NT):
                    act.wait_ge(o_out, h * 4 + (t + 1))
                    if t > 0:
                        act.wait_ge(sq_ok, h * NT + (NT + t))
                    act.activation(o_sq, o_sb[:, t], ACT.Square, accum_out=stat[:, 0, t:t + 1])\
                        .then_inc(sq_ok, 1)
                rsqrt(h + 2, NT)

            n0 = st.n
            gla_head(0, True)
            per = st.n - n0
            with act.Fori(1, G_HEADS) as h:
                st.enter(h - 1, per)
                gla_head(h, False)
                st.leave(G_HEADS - 1)

            def load_residual(j):
                act.wait_ge(x1_ok, j * NT)
                for t in range(NT):
                    src = io["x"][0] if t < C0 else io["ctx"][0]
                    act.dma_start(xres[:, t], src[(t % 2) * P:(t % 2 + 1) * P, bass.ds(j * CW, CW)])\
                        .then_inc(xres_in, 16)

            act.wait_ge(u_ok, NT * G_HEADS)
            load_residual(0)
            high_parts(1, hfu, OUT0)
            with act.Fori(1, 4) as j:
                splits(j + OUT0, range(4))
                load_residual(j)
                splits(j + OUT0, range(4, 8))
            splits(DIFF, range(4))
            act.wait_ge(x1_ok, 4 * NT)
            row_squares()
            rsqrt(G_HEADS + 2, NT)
            high_parts(2, hf, DIFF)

            def softmax(h):
                for i in range(4):
                    act.wait_ge(max_ok, h * 4 + (i + 1))
                    act.activation(probs[:, i // 2, i % 2], bank[4 + i][:], ACT.Exp, bias=smx[:, 0, i:i + 1],
                                   scale=A_D ** -0.5, accum_out=smx[:, 1, i:i + 1]).then_inc(p_ok, 1)

            BATCH = G_HEADS + 2

            def attention_head(h, before):
                c = h * 2 + DIFF
                if before:
                    splits(c, range(4, 7))
                    softmax(h - 1)
                    splits(c, range(7, 8))
                splits(c + 1, range(0, 3))
                if before:
                    rsqrt(h * 3 + BATCH, 2)
                splits(c + 1, range(3, 4))
                rsqrt(h * 3 + (BATCH + 1), 8)
                splits(c + 1, range(4, 8))
                splits(c + 2, range(0, 4))
                for t in range(2):
                    act.wait_ge(freed[t], h * 2 + (DIFF + 2))
                act.activation(silu_ag, qg[:, :, A_DV:CW], ACT.Silu).then_inc(g_ok, 1)
                rsqrt(h * 3 + (BATCH + 2), 4)

            act.wait_ge(acts_ok, 3 * NK)
            for i, name in enumerate(("cos", "sin", "cos", "sin")):
                act.dma_start(rope[:, i], io[name].rearrange("(t p) n -> p t n", p=P)).then_inc(rows_in, 16)
            act.dma_start(knw, io["diff_kn_w"][0].rearrange("m n -> (m n)").partition_broadcast(P))\
                .then_inc(rows_in, 16)
            act.dma_start(silu_ag[:, 0], io["diff_qn_w"][0].rearrange("m n -> (m n)").partition_broadcast(P))\
                .then_inc(rows_in, 16)
            act.wait_ge(rope_ok, 1)
            attention_head(0, False)
            with act.Fori(1, A_HEADS) as h:
                st.enter(h - 1, 3)
                attention_head(h, True)
                st.leave(A_HEADS - 1)
            softmax(A_HEADS - 1)
            rsqrt(A_HEADS * 3 + BATCH, 2)
            high_parts(3, hfu, OUT1)

            def store(j):
                act.wait_ge(y_ok, j * 2 + 2)
                for t in range(2):
                    act.dma_start(out[0][t * P:(t + 1) * P, bass.ds(j * CW, CW)], yrow[:, t]).then_inc(y_out, 16)

            with act.Fori(1, 4) as j:
                splits(j + OUT1, range(4))
                store(j - 1)
                splits(j + OUT1, range(4, 8))
            store(3)
            act.wait_ge(y_out, 4 * 2 * 16)

        @block.tensor
        def _(pe):
            def modulation_tile(b, w, k):
                for n in range(4):
                    last = pe.matmul(b[:, 2 * n:2 * n + 2], w[:, n * P:(n + 1) * P], silu_c[:, k, :],
                                     start=(k == 0 and n == 0), stop=False, skip_group_check=True)
                return last

            def modulation_sum(b, acc, first=True):
                for n in range(4):
                    for m in range(2):
                        last = pe.matmul(b[:, 2 * n + m:2 * n + m + 1], acc[:, m, n * P:(n + 1) * P],
                                         ones[:, 0:1], start=(first and n == 0 and m == 0), stop=True,
                                         skip_group_check=True)
                last.then_inc(mod_sum, 1)

            def background(c, acc):
                pe.wait_ge(ada_used, c * NK + (NK + 2))
                pe.wait_ge(ada_taken, c + STARTUP)
                modulation_sum(bank[7], acc)

            def project(c, frees, rows_stationary, tiles=NT, before=None, after=None):
                for p in range(PAIRS):
                    if before is not None:
                        before(p)
                    pe.wait_ge(w_split, c * PAIRS + (p + 1 + RING))
                    for j in range(2):
                        k, wh, wl = 2 * p + j, w_hi[:, p % RING, j], w_lo[:, p % RING, j]
                        for t in range(tiles):
                            if k == 0:
                                pe.wait_ge(freed[t], frees(t))
                            x = slice(t * P, (t + 1) * P)
                            if rows_stationary:
                                ops = ((hi[:, k, x], wl), (hi[:, k, x], wh), (lo[:, k, x], wh))
                            else:
                                ops = ((wl[:, x], hi[:, k, :]), (wh[:, x], hi[:, k, :]), (wh[:, x], lo[:, k, :]))
                            for i, (a, b) in enumerate(ops):
                                last = pe.matmul(bank[t][:], a, b, start=(k == 0 and i == 0),
                                                 stop=(k == NK - 1 and i == 2))
                            if k == NK - 1 and t < tiles - 1:
                                last.then_inc(acc_ok, 1)
                        if j == 1:
                            last.then_inc(pair_done, 1)
                    if after is not None:
                        after(p)

            def transpose_tile(stage, src, k, n=NT):
                if k >= 3:
                    pe.wait_ge(hf_ok, stage * NK + k - 2)
                for t in range(n):
                    last = pe.transpose(bank[4 + k % 3][:, t * P:(t + 1) * P], src[:, t, k * P:(k + 1) * P], ident[:])
                last.then_inc(xt_ok, 1)

            def transposing(stage, src, n=NT):
                def before(p):
                    for k in range(4) if p == 0 else range(4 if p == 1 else 2 * p + 4, min(2 * p + 6, NK)):
                        transpose_tile(stage, src, k, n)
                    pe.wait_ge(acts_ok, stage * NK + 2 * p + 2)
                return before

            pe.wait_ge(vec_in, 16 * 8)
            pe.wait_ge(const_in, CONSTS)
            pe.transpose(bank[4][:, 0:V_ROWS], vec1[0:V_ROWS, :], ident[0:V_ROWS, 0:V_ROWS]).then_inc(cols_t, 1)
            pe.transpose(bank[5][:, 0:96], vec2[0:96, :], ident[0:96, 0:96]).then_inc(cols_t, 1)
            pe.wait_ge(lam_pr_ok, 1)
            pe.matmul(bank[4][:, 0:2], ones[:], lam_pr, start=True, stop=True).then_inc(lam_t, 1)
            pe.wait_ge(silu_ok, 2)

            def startup_chunk(a, odd, first):
                b = bank[7 - odd]
                for p in range(PAIRS - 1):
                    pe.wait_ge(raw_in[p % RING], a * 32 + 16 * (p // RING + 1))
                    if p == 0 and not first:
                        pe.wait_ge(ada_taken, a - 1)
                    modulation_tile(b, raw[:, p % RING, 0], 2 * p).then_inc(ada0_pe, 1 if p < PAIRS - 2 else 2)
                pe.wait_ge(ada0_dve, a * PAIRS + PAIRS)
                modulation_sum(b, startup_acc[odd], first=False)

            startup_chunk(0, 0, True)
            startup_chunk(1, 1, True)
            with pe.Fori(1, STARTUP // 2) as i:
                startup_chunk(i * 2, 0, False)
                startup_chunk(i * 2 + 1, 1, False)

            def gate_columns():
                pe.wait_ge(a1_ok, 1)
                for t in range(NT):
                    for k in range(NK):
                        x = slice(t * P, (t + 1) * P)
                        pe.matmul(bank[4][:, t * 64:(t + 1) * 64], hi[:, k, x], a1[:, k].rearrange("p a b -> p (a b)"),
                                  start=(k == 0), stop=False, skip_group_check=True)
                        last = pe.matmul(bank[4][:, t * 64:t * 64 + 32], lo[:, k, x], a1[:, k, 0],
                                         start=False, stop=(k == NK - 1), skip_group_check=True)
                last.then_inc(z_ok, 1)
                pe.wait_ge(z_sb_ok, 1)
                for dr in range(2):
                    for t in range(NT):
                        last = pe.transpose(bank[5 + dr][0:G_RANK, t * P:(t + 1) * P],
                                            z_sb[:, t, dr * G_RANK:(dr + 1) * G_RANK], ident[:])
                    last.then_inc(zt_ok, 1)
                pe.wait_ge(zT_ok, 2)

            def gate_logits(h):
                pe.wait_ge(a2_in, h * 32 + 32)
                for n in range(4):
                    dr = 1 if n < 2 else 0
                    rows = slice(32 * dr, 32 * dr + G_RANK)
                    if n == 3:
                        pe.wait_ge(logit_out, h * 4 + 1)
                    elif n == 0:
                        pe.wait_ge(o_out, h * 4)
                    pe.matmul(bank[4 + n % 3][:], a2[rows, (n % 2) * P:(n % 2 + 1) * P], zT[rows, :],
                              start=True, stop=True).then_inc(logit_ok, 1)

            def score(out_, k_part, q_part, start=False):
                return pe.matmul(out_, k_part, q_part, start=start, stop=True, skip_group_check=True)

            DIAG = {X0: (6, 0), X1: (6, 384), C0: (4, 256), C1: (5, 384)}

            def tok(v, t, n=P, at_=0):
                return v[:, t * P + at_:t * P + at_ + n]

            def unit_scores(h, n):
                pe.wait_ge(til_ok, h * 4 + (n + 1))
                back, first = n < 2, n == 0
                score(bank[4][:, 0:256], tok(kb, C0), qB if back else qA, first)
                score(bank[5][:, 0:256], tok(kb, C1), qA if back else qB, first)
                if back:
                    score(bank[6][:, 256:384], tok(kb, X1), tok(qh, X0), first)
                    score(bank[5][:, 256:384], tok(kb, C1), tok(qh, C0))
                else:
                    score(bank[6][:, 128:256], tok(kb, X0), tok(qh, X1))
                    score(bank[4][:, 384:512], tok(kb, C0), tok(qh, C1))
                for t in range(NT):
                    b, at_ = DIAG[t]
                    low, high = slice(0, HALF), slice(HALF, P)
                    if back:
                        score(bank[b][high, at_:at_ + HALF], k1[:, t], q1[:, t])
                        col = 256 + t * HALF
                        score(bank[7][low, col:col + HALF], tok(k2, t, HALF), tok(q2, t, HALF))
                        last = score(bank[7][high, col:col + HALF], tok(k2, t, HALF, HALF), tok(q2, t, HALF, HALF))
                    else:
                        score(bank[b][low, at_ + HALF:at_ + P], k1[:, t], q1[:, t])
                        score(bank[b][low, at_:at_ + HALF], tok(k2, t, HALF), tok(q2, t, HALF))
                        last = score(bank[b][high, at_ + HALF:at_ + P], tok(k2, t, HALF, HALF),
                                     tok(q2, t, HALF, HALF))
                last.then_inc(unit_done, 1)

            READ = {X0: ((C0, 0, 0), (C1, 1, 0), (X0, 2, 0), (X1, 2, 256)),
                    X1: ((C0, 0, 128), (C1, 1, 128), (X0, 2, 128), (X1, 2, 384)),
                    C0: ((C0, 0, 256), (C1, 1, 256)),
                    C1: ((C0, 0, 384), (C1, 1, 384))}

            def head_outputs(h):
                pe.wait_ge(at_ok, h + 1)
                for t in range(NT):
                    if t == 3:
                        pe.wait_ge(o_out, h * 4 + 1)
                    for i, (kt, b, col) in enumerate(READ[t]):
                        last = pe.matmul(bank[4 + t % 3][:], at[:, b, col:col + P], v_sb[:, kt, :],
                                         start=(i == 0), stop=(i == len(READ[t]) - 1))
                    last.then_inc(o_ok, 1)

            def gla_head(h, before=None, gates=None):
                c = h * 3
                project(c, lambda t: c, False, before=before)
                background(c, mod_acc_g)
                if gates is not None:
                    gates()
                gate_logits(h)
                project(c + 1, lambda t: c + 1, True,
                        after=lambda p: unit_scores(h, 0) if p == 5 else None)

                def after(p):
                    if p == 2:
                        pe.wait_ge(d2_ok, h + 1)
                        background(c + 1, mod_acc_v)
                    if p in (0, 3, 6):
                        unit_scores(h, {0: 1, 3: 2, 6: 3}[p])

                project(c + 2, lambda t: c + 2, True, after=after)
                background(c + 2, mod_acc_g)
                head_outputs(h)

            pe.wait_ge(xn_ok, NT)
            pe.wait_ge(ada_taken, STARTUP)
            gla_head(0, before=transposing(0, xn), gates=gate_columns)
            with pe.Fori(1, G_HEADS) as h:
                gla_head(h)

            def gate_rows(first, batches):
                for n in range(first, first + batches):
                    pe.wait_ge(diag_ok, n + 1)
                    if n >= first + 2:
                        pe.wait_ge(gate_ok, n - 1)
                    pe.matmul(bank[5 + n % 2][:], ones[:], diag4[n % 2].rearrange("p a b -> p (a b)"),
                              start=True, stop=True).then_inc(gate_t, 1)

            pe.wait_ge(u_ok, NT * G_HEADS)
            gate_rows(0, 8)
            pe.wait_ge(gate_ok, 8)
            project(OUT0, lambda t: OUT0, True, before=transposing(1, u))
            background(OUT0, mod_acc)
            with pe.Fori(OUT0 + 1, DIFF) as c:
                project(c, lambda t: c, True)
                background(c, mod_acc)

            def frees(h, second):
                def of(t):
                    return h * 2 + (DIFF + second) if t < 2 else h + DIFF
                return of

            def key_transposes(h):
                pe.wait_ge(k_ok, h + 1)
                for m in range(2):
                    for t in range(NT):
                        last = pe.transpose(bank[4 + m][:, t * P:(t + 1) * P], k_n[:, t, m * P:(m + 1) * P], ident[:])
                    last.then_inc(kt_t, 1)

            def query_transposes(h):
                pe.wait_ge(q_ok, h + 1)
                for m in range(2):
                    for t in range(2):
                        last = pe.transpose(bank[6][:, (2 * m + t) * P:(2 * m + t + 1) * P],
                                            q_t[:, t, m * P:(m + 1) * P], ident[:])
                last.then_inc(qt_t, 1)

            def attention_scores(h):
                pe.wait_ge(qT_ok, h + 1)
                pe.wait_ge(kT_ok, h * 2 + 2)
                for i in range(4):
                    t, m = i // 2, i % 2
                    pe.matmul(bank[4 + i][:], qT[:, m, t * P:(t + 1) * P], kT[:, m, :], start=True, stop=True)\
                        .then_inc(s_ok, 1)

            def weight_transposes(h):
                pe.wait_ge(a_ok, h * 2 + 2)
                for b in range(2):
                    for kt in (2 * b, 2 * b + 1):
                        for t in range(2):
                            at_ = (kt % 2) * 256 + t * P
                            last = pe.transpose(bank[4 + b][:, at_:at_ + P], probs[:, t, 0, kt * P:(kt + 1) * P], ident[:])
                    last.then_inc(at_t, 1)

            def attention_outputs(h):
                pe.wait_ge(aT_ok, h * 2 + 2)
                for t in range(2):
                    for kt in range(NT):
                        last = pe.matmul(bank[6][:, t * A_DV:(t + 1) * A_DV], aT[:, kt, t * P:(t + 1) * P],
                                         kv[:, kt, A_DV:CW], start=(kt == 0), stop=(kt == NT - 1))
                last.then_inc(pv_ok, 1)

            def attention_head(h, before=None, behind=None):
                c = h * 2 + DIFF
                project(c, frees(h, 0), True, before=before,
                        after=None if behind is None else lambda p: behind[p](h - 1) if p in behind else None)
                project(c + 1, frees(h, 1), True, tiles=2,
                        after=lambda p: key_transposes(h) if p == 5 else None)

            pe.wait_ge(xn_ok, 2 * NT)
            attention_head(0, before=transposing(2, xn))
            with pe.Fori(1, A_HEADS) as h:
                attention_head(h, behind={1: query_transposes, 2: attention_scores, 5: weight_transposes,
                                          6: attention_outputs})
            for step in (query_transposes, attention_scores, weight_transposes, attention_outputs):
                step(A_HEADS - 1)
            pe.wait_ge(u_ok, NT * G_HEADS + 2 * A_HEADS)
            gate_rows(8, 4)
            pe.wait_ge(gate_ok, 12)
            project(OUT1, lambda t: OUT1, True, tiles=2, before=transposing(3, u1, 2))
            with pe.Fori(OUT1 + 1, CHUNKS) as c:
                project(c, lambda t: c, True, tiles=2)

        @block.vector
        def _(dve):
            st = Steps(dve, dve_step)

            def complete(n, c, t, tiles=NT):
                if t == tiles - 1:
                    dve.wait_ge(pair_done, c * PAIRS + (PAIRS + RING))
                else:
                    dve.wait_ge(acc_ok, n + (t + 1))

            def newton(width):
                v, r, s = (stat[:, i, 0:width] for i in (1, 2, 3))
                st.step(dve.tensor_tensor(s, r, r, ALU.mult))
                st.wait()
                st.step(dve.tensor_tensor(s, s, v, ALU.mult))
                st.wait()
                st.step(dve.tensor_scalar(s, s, -0.5, 1.5, ALU.mult, ALU.add))
                st.wait()
                st.step(dve.tensor_tensor(r, r, s, ALU.mult))
                st.wait()

            def inverse_rms(n, width, count):
                dve.tensor_scalar(stat[:, 1, 0:width], stat[:, 0, 0:width], 1.0 / count, EPS, ALU.mult, ALU.add)\
                    .then_inc(mean_ok, 1)
                dve.wait_ge(rs_ok, n)
                newton(width)

            dve.wait_ge(cols_t, 1)
            dve.tensor_copy(cols1[:], bank[4][:, 0:V_ROWS]).then_inc(cols_ok, 1)
            dve.wait_ge(cols_t, 2)
            dve.tensor_copy(cols2[:], bank[5][:, 0:96]).then_inc(cols_ok, 1)
            dve.wait_ge(cols_ok, 2)
            lv = cols1[:, V_LAM:V_LAM + 4].rearrange("p (a b) -> p a b", b=2)
            dve.tensor_tensor(lam_pr, lv[:, :, 0], lv[:, :, 1], ALU.mult).then_inc(lam_pr_ok, 1)
            st.step(dve.tensor_scalar(cols1[:, V_SUB:V_SUB + 2], cols1[:, V_SUB:V_SUB + 2], 1.0 - LAMBDA_INIT,
                                      None, ALU.mult))
            dve.wait_ge(lam_e, 1)
            st.step(dve.tensor_tensor(lam[:, 2:3], lam[:, 0:1], lam[:, 1:2], ALU.subtract))
            st.wait()
            st.step(dve.tensor_scalar(lam[:, 3:4], lam[:, 2:3], LAMBDA_INIT, None, ALU.add))

            def row_norm(n):
                dve.wait_ge(sq_ok, NT if n == 1 else NT + NT * G_HEADS + NT)
                inverse_rms(n, NT, D)
                for t in range(NT):
                    dve.tensor_scalar(xn[:, t, :], u[:, t, :], stat[:, 2, t:t + 1], None, ALU.mult).then_inc(xn_ok, 1)

            def weigh(acc, w, k, first):
                def one(m):
                    s = silu_c[:, k, m:m + 1]
                    if first:
                        return dve.tensor_scalar(acc[:, m], w, s, None, ALU.mult)
                    return dve.scalar_tensor_tensor(acc[:, m], w, s, acc[:, m], ALU.mult, ALU.add)

                if not first:
                    st.wait()
                st.step(one(0))
                return one

            def startup_tiles(a, odd):
                acc = startup_acc[odd]
                for p in range(PAIRS):
                    dve.wait_ge(raw_in[p % RING], a * 32 + 16 * (p // RING + 1))
                    if p == PAIRS - 1:
                        one = weigh(acc, raw[:, p % RING, 0], 2 * p, False)
                        dve.wait_ge(ada0_dve, a * PAIRS + p)
                        st.step(one(1))
                    one = weigh(acc, raw[:, p % RING, 1], 2 * p + 1, p == 0)
                    if p == PAIRS - 1:
                        st.wait()
                    elif p > 0:
                        dve.wait_ge(ada0_dve, a * PAIRS + p)
                    one(1).then_inc(ada0_dve, 1)

            def background_tiles(c, acc, ks):
                for k in ks:
                    dve.wait_ge(ada_in[k % 2], c * (8 * 16) + 16 * (k // 2 + 1))
                    one = weigh(acc, ada_w[:, k % 2], k, k == 0)
                    if k > 0:
                        dve.wait_ge(ada_used, c * NK + (k + 2))
                    one(1).then_inc(ada_used, 1)

            def take_modulation(s, tile0, c, b=bank[7]):
                dve.wait_ge(mod_sum, c + 1)
                tiles = bass.ds(tile0 + s * NK, 4)
                dve.tensor_tensor(mod[:].rearrange("p s k m -> p (s k) m")[:, tiles],
                                  b[:, 0:8].rearrange("p (n m) -> p n m", m=2),
                                  cols2[:, tiles].unsqueeze(2).broadcast_to([P, 4, 2]), ALU.add).then_inc(ada_taken, 1)

            def scale_columns(layer, taken):
                dve.wait_ge(ada_taken, taken)
                s = mod[:, 3 * layer + 1]
                w = cols1[:, V_NORM + layer * NK:V_NORM + (layer + 1) * NK].unsqueeze(2).broadcast_to([P, NK, 2])
                st.step(dve.scalar_tensor_tensor(s, s, 1.0, w, ALU.add, ALU.mult))
                st.wait()

            dve.wait_ge(silu_ok, 2)
            startup_tiles(0, 0)
            dve.wait_ge(a1_hi_ok, 1)
            dve.tensor_tensor(a1[:, :, 1], a1_raw, a1[:, :, 0].bitcast(F32), ALU.subtract).then_inc(a1_ok, 1)
            startup_tiles(1, 1)
            take_modulation(0, 0, 0)
            row_norm(1)
            with dve.Fori(1, STARTUP // 2) as i:
                st.enter(i - 1, 2 * (PAIRS + 2))
                startup_tiles(i * 2, 0)
                take_modulation(0, i * 8 - 4, i * 2 - 1, bank[6])
                startup_tiles(i * 2 + 1, 1)
                take_modulation(0, i * 8, i * 2)
                st.leave(STARTUP // 2 - 1)
            take_modulation(0, 4 * (STARTUP - 1), STARTUP - 1, bank[6])
            scale_columns(0, STARTUP)

            def modulated(layer):
                def emit(k, dst, src):
                    for m in range(2):
                        x = slice(m * 2 * P, (m + 1) * 2 * P)
                        last = dve.tensor_scalar(dst[:, x], src[:, x], mod[:, 3 * layer + 1, k, m:m + 1],
                                                 mod[:, 3 * layer, k, m:m + 1], ALU.mult, ALU.add)
                    return last
                return emit

            def weighted(col0, n, width):
                def emit(k, dst, src):
                    return dve.tensor_scalar(dst[:, 0:width], src[:, 0:width], cols1[:, col0 + k % n:col0 + k % n + 1],
                                             None, ALU.mult)
                return emit

            def activation_tiles(stage, buf, emit, width=TOK, beside=None):
                def low(k):
                    dve.wait_ge(hi_ok, stage * NK + k + 1)
                    dve.tensor_tensor(lo[:, k, 0:width], buf[:, k % 2, 0:width], hi[:, k, 0:width].bitcast(F32),
                                      ALU.subtract).then_inc(acts_ok, 1)

                for k in range(NK):
                    dve.wait_ge(xt_ok, stage * NK + k + 1)
                    if k > 1:
                        dve.wait_ge(acts_ok, stage * NK + k - 1)
                    emit(k, buf[:, k % 2], bank[4 + k % 3]).then_inc(hf_ok, 1)
                    if k > 0:
                        low(k - 1)
                    if beside is not None:
                        beside(k)
                low(NK - 1)

            dve.wait_ge(xn_ok, NT)
            activation_tiles(0, hf, modulated(0), beside=lambda k: background_tiles(0, mod_acc_g, [k]))

            dve.wait_ge(const_in, CONSTS)

            def tokens(v, n):
                return v.rearrange("p (t s) -> p t s", s=n)

            def unit_tildes(h, n, meanwhile=None):
                back = n < 2
                b = bcum[:, n, :]
                b64, b128 = tokens(b, HALF), tokens(b, P)
                mid, split_at, tot = (HALF // 2, HALF, 0) if back else (HALF // 2 - 1, HALF - 1, P - 1)
                near, far = (slice(0, HALF), slice(HALF, P)) if back else (slice(HALF, P), slice(0, HALF))
                if n > 0:
                    dve.wait_ge(unit_done, h * 4 + n)
                dve.tensor_tensor(tokens(q2, HALF), b64, b64[:, :, mid:mid + 1].broadcast_to([P, 8, HALF]), ALU.subtract)
                dve.tensor_tensor(tokens(kb, P), b128, b128[:, :, tot:tot + 1].broadcast_to([P, NT, P]), ALU.subtract)
                ref = b128[:, :, split_at:split_at + 1].broadcast_to([P, NT, HALF])
                dve.tensor_tensor(q1, b128[:, :, near], ref, ALU.subtract)
                dve.tensor_tensor(k1, b128[:, :, far], ref, ALU.subtract).then_inc(d_ok, 1)
                q, k = qkT[:, n % 2, :], qkT[:, 2 + n % 2, :]
                if meanwhile is not None:
                    background_tiles(*meanwhile)
                dve.wait_ge(e_ok, h * 4 + (n + 1))
                st.step(dve.tensor_tensor(qh, qh, q, ALU.mult))
                dve.tensor_tensor(kb, kb, k, ALU.mult)
                dve.tensor_tensor(q2, q2, q, ALU.mult)
                dve.tensor_tensor(k2, k2, k, ALU.mult)
                dve.tensor_tensor(q1, q1, tokens(q, P)[:, :, near], ALU.mult)
                dve.tensor_tensor(k1, k1, tokens(k, P)[:, :, far], ALU.mult)
                st.wait()
                one, two, between = (X1, X0, C0) if back else (X0, X1, C1)
                dve.tensor_copy(qB[:, one * P:(one + 1) * P], qh[:, one * P:(one + 1) * P])
                st.step(dve.tensor_scalar(qB[:, two * P:(two + 1) * P], qh[:, two * P:(two + 1) * P],
                                          g_tot[:, one:one + 1], None, ALU.mult))
                st.wait()
                dve.tensor_scalar(qA, qB, g_tot[:, between:between + 1], None, ALU.mult).then_inc(til_ok, 1)

            DIAG = {X0: (2, 0), X1: (2, 384), C0: (0, 256), C1: (1, 384)}

            def gla_head(h, first):
                c = h * 3
                if not first:
                    background_tiles(c, mod_acc_g, range(NK))
                for t in range(NT):
                    complete(h * 9, c, t)
                    if t < 2:
                        dve.tensor_scalar(qkT[:, t], bank[t][:], G_DK ** -0.5, None, ALU.mult).then_inc(freed[t], 1)
                    else:
                        dve.tensor_copy(qkT[:, t], bank[t][:]).then_inc(freed[t], 1)
                take_modulation(2, h * 4, c + STARTUP)
                if first:
                    dve.wait_ge(z_ok, 1)
                    z = bank[4][:, 0:NT * 64].rearrange("p (t a r) -> p t a r", t=NT, a=2)
                    st.step(dve.tensor_copy(z_sb, z[:, :, 0]))
                    st.wait()
                    dve.tensor_tensor(z_sb, z_sb, z[:, :, 1], ALU.add).then_inc(z_sb_ok, 1)
                    for dr in range(2):
                        dve.wait_ge(zt_ok, dr + 1)
                        dve.tensor_copy(zT[32 * dr:32 * dr + G_RANK, :], bank[5 + dr][0:G_RANK, :]).then_inc(zT_ok, 1)
                else:
                    dve.wait_ge(u_ok, h * NT)
                for n in range(4):
                    dve.wait_ge(logit_ok, h * 4 + (n + 1))
                    dr = 1 if n < 2 else 0
                    bias = cols1[:, bass.ds(h * 2 + (V_GATEB + 8 * dr + n % 2), 1)]
                    dve.tensor_scalar(bcum[:, n], bank[4 + n % 3][:], bias, None, ALU.add).then_inc(logit_out, 1)
                background_tiles(c + 1, mod_acc_v, range(0, 2))
                for n in range(4):
                    dve.wait_ge(ln_ok, h * 4 + (n + 1))
                    st.step(dve.scalar_tensor_tensor(ln_t[:, n], bcum[:, n], 0.0, ln_t[:, n], ALU.min, ALU.subtract))
                    background_tiles(c + 1, mod_acc_v, [n + 2])
                    st.wait()
                    for t in range(NT):
                        src, dst = ln_t[:, n, t * P:(t + 1) * P], bcum[:, n, t * P:(t + 1) * P]
                        if n < 2:
                            src, dst = src[:, ::-1], dst[:, ::-1]
                        last = dve.tensor_tensor_scan(dst, ones[:], src, 0.0, ALU.mult, ALU.add)
                st.step(last)
                st.wait()
                unit_tildes(h, 0, (c + 1, mod_acc_v, range(6, 9)))
                background_tiles(c + 1, mod_acc_v, range(9, 11))
                unit_tildes(h, 1, (c + 1, mod_acc_v, range(11, 14)))
                for t in range(NT):
                    complete(h * 9 + 3, c + 1, t)
                    dve.tensor_copy(v_sb[:, t], bank[t][:]).then_inc(freed[t], 1)
                background_tiles(c + 1, mod_acc_v, range(14, NK))
                background_tiles(c + 2, mod_acc_g, range(0, 2))
                unit_tildes(h, 2, (c + 2, mod_acc_g, range(2, 5)))
                d2 = bank[7][:, 256:512].rearrange("p (t s) -> p t s", s=HALF)
                for half in range(2):
                    r = slice(half * HALF, (half + 1) * HALF)
                    last = dve.copy_predicated(d2m[r, :, r], mask2[r].unsqueeze(1).broadcast_to([HALF, NT, HALF]), d2[r])
                last.then_inc(d2_ok, 1)
                background_tiles(c + 2, mod_acc_g, range(5, 8))
                take_modulation(3, h * 4, c + (STARTUP + 1))
                unit_tildes(h, 3, (c + 2, mod_acc_g, range(8, 11)))
                background_tiles(c + 2, mod_acc_g, range(11, NK))
                dve.wait_ge(unit_done, h * 4 + 4)
                dve.tensor_copy(at[:, 0, 0:256], bank[4][:, 0:256])
                for t in range(NT):
                    b, col = DIAG[t]
                    last = dve.copy_predicated(d1m[:, t, :], mask1[:], bank[4 + b][:, col:col + P])
                st.step(last)
                dve.tensor_copy(at[:, 0, 384:512], bank[4][:, 384:512])
                dve.tensor_copy(at[:, 1, 0:384], bank[5][:, 0:384])
                dve.tensor_copy(at[:, 2, 128:384], bank[6][:, 128:384])
                st.wait()
                for t in range(NT):
                    b, col = DIAG[t]
                    last = dve.tensor_tensor(at[:, b, col:col + P], d1m[:, t, :], d2m[:, t, :], ALU.add)
                last.then_inc(at_ok, 1)
                take_modulation(4, h * 4, c + (STARTUP + 2))
                for t in range(NT):
                    dve.wait_ge(o_ok, h * 4 + (t + 1))
                    dve.tensor_copy(o_sb[:, t], bank[4 + t % 3][:]).then_inc(o_out, 1)
                dve.wait_ge(sq_ok, h * NT + 2 * NT)
                inverse_rms(h + 2, NT, G_DV)
                for t in range(NT):
                    dve.scalar_tensor_tensor(u[:, t, bass.ds(h * G_DV, G_DV)], o_sb[:, t], stat[:, 2, t:t + 1],
                                             silu_g[:, t], ALU.mult, ALU.mult).then_inc(u_ok, 1)

            n0 = st.n
            gla_head(0, True)
            per = st.n - n0 - 1 + NK
            with dve.Fori(1, G_HEADS) as h:
                st.enter(h - 1, per)
                gla_head(h, False)
                st.leave(G_HEADS - 1)

            def gate_rows(s, cond, batch0):
                def diagonals(i):
                    n = batch0 + i
                    if n > 1:
                        dve.wait_ge(gate_t, n - 1)
                    dve.tensor_tensor(diag4[n % 2], ident[:].unsqueeze(1).broadcast_to([P, 4, P]),
                                      mod[:, s, 4 * i:4 * i + 4, cond:cond + 1].broadcast_to([P, 4, P]), ALU.mult)\
                        .then_inc(diag_ok, 1)

                diagonals(0)
                for i in range(4):
                    if i < 3:
                        diagonals(i + 1)
                    n = batch0 + i
                    dve.wait_ge(gate_t, n + 1)
                    dve.tensor_copy(gate_row[:, cond, i * CW:(i + 1) * CW], bank[5 + n % 2][:]).then_inc(gate_ok, 1)

            dve.wait_ge(u_ok, NT * G_HEADS)
            dve.wait_ge(ada_taken, STARTUP + OUT0)
            gate_rows(2, 0, 0)
            gate_rows(2, 1, 4)
            activation_tiles(1, hfu, weighted(V_GN, G_DV // P, TOK),
                             beside=lambda k: background_tiles(OUT0, mod_acc, [k]))

            def after_layer0(j, first):
                c = j + OUT0
                if not first:
                    background_tiles(c, mod_acc, range(NK))
                dve.wait_ge(xres_in, j * 64 + 64)
                for t in range(NT):
                    complete(j * 3 + 3 * OUT0, c, t)
                    dve.tensor_tensor(yrow[:, t], bank[t][:], gate_row[:, t // 2, bass.ds(j * CW, CW)], ALU.mult)\
                        .then_inc(freed[t], 1)
                    dve.wait_ge(freed[t], c + 1)
                    dve.tensor_tensor(u[:, t, bass.ds(j * CW, CW)], yrow[:, t], xres[:, t], ALU.add).then_inc(x1_ok, 1)
                take_modulation(5, j * 4, c + STARTUP)

            after_layer0(0, True)
            with dve.Fori(1, 4) as j:
                st.enter(j - 1, NK)
                after_layer0(j, False)
                st.leave(3)

            row_norm(G_HEADS + 2)
            scale_columns(1, STARTUP + DIFF)
            activation_tiles(2, hf, modulated(1))

            dve.wait_ge(rows_in, 16 * 6)

            def swapped(dst, src, tab):
                def g(v):
                    return v.rearrange("p t (g a s) -> p t g a s", a=2, s=32)
                for a in range(2):
                    last = dve.tensor_tensor(g(dst)[:, :, :, a], g(src)[:, :, :, 1 - a], g(tab)[:, :, :, a], ALU.mult)
                return last

            for i, w in ((0, silu_ag[:, 0]), (2, knw)):
                for t in range(2):
                    dve.tensor_tensor(rope[:, i, t], rope[:, i, t], w, ALU.mult)
                    last = swapped(rope[:, i + 1, t:t + 1], w.unsqueeze(1), rope[:, i + 1, t:t + 1])
            last.then_inc(rope_ok, 1)
            dve.wait_ge(rope_ok, 1)

            def flat(v):
                return v.rearrange("p a b -> p (a b)")

            def rotate(n, tmp, i, normed_into):
                a, b = tmp
                dve.tensor_tensor(a, n, rope[:, i], ALU.mult)
                st.step(swapped(b, n, rope[:, i + 1]))
                st.wait()
                return dve.tensor_tensor(normed_into, a, b, ALU.add)

            def squares(dst, src, groups):
                st.step(dve.tensor_tensor(dst, src, src, ALU.mult))
                st.wait()
                st.step(dve.tensor_reduce(stat[:, 0, 0:groups],
                                          flat(dst).rearrange("p (g d) -> p g d", g=groups), AX.X, ALU.add))
                st.wait()

            BATCH = G_HEADS + 2

            def keys(h):
                c = h * 2 + DIFF
                for t in range(NT):
                    complete(h * 4 + 3 * DIFF, c, t)
                    dve.tensor_copy(kv[:, t], bank[t][:]).then_inc(freed[t], 1)
                dve.wait_ge(freed[3], h + DIFF + 1)
                k_raw = kv[:, :, 0:256]
                squares(k_t, k_raw, 8)
                inverse_rms(h * 3 + (BATCH + 1), 8, A_D)
                rs = stat[:, 2, 0:8].rearrange("p (t m) -> p t m", m=2)
                for m in range(2):
                    last = dve.tensor_tensor(k_n[:, :, m * P:(m + 1) * P], k_raw[:, :, m * P:(m + 1) * P],
                                             rs[:, :, m:m + 1].broadcast_to([P, NT, P]), ALU.mult)
                st.step(last)
                st.wait()
                dve.tensor_tensor(k_n[:, 2:4], k_n[:, 2:4], knw.unsqueeze(1).broadcast_to([P, 2, 256]), ALU.mult)
                rotate(k_n[:, 0:2], (k_t[:, 0:2], k_t[:, 2:4]), 2, k_n[:, 0:2]).then_inc(k_ok, 1)
                for m in range(2):
                    dve.wait_ge(kt_t, h * 2 + (m + 1))
                    dve.tensor_copy(kT[:, m], bank[4 + m][:]).then_inc(kT_ok, 1)

            def queries(h):
                c = h * 2 + (DIFF + 1)
                for t in range(2):
                    complete(h * 4 + (3 * DIFF + 3), c, t, 2)
                    dve.tensor_copy(qg[:, t], bank[t][:]).then_inc(freed[t], 1)
                dve.wait_ge(freed[1], h * 2 + (DIFF + 2))
                q_raw = qg[:, :, 0:256]
                squares(q_t, q_raw, 4)
                inverse_rms(h * 3 + (BATCH + 2), 4, A_D)
                rs = stat[:, 2, 0:4].rearrange("p (t m) -> p t m", m=2)
                for m in range(2):
                    last = dve.tensor_tensor(q_raw[:, :, m * P:(m + 1) * P], q_raw[:, :, m * P:(m + 1) * P],
                                             rs[:, :, m:m + 1].broadcast_to([P, 2, P]), ALU.mult)
                st.step(last)
                st.wait()
                rotate(q_raw, (q_t, q_u), 0, q_t).then_inc(q_ok, 1)

            def attend(h):
                dve.wait_ge(qt_t, h + 1)
                dve.tensor_copy(qT.rearrange("p m n -> p (m n)"), bank[6][:]).then_inc(qT_ok, 1)
                for i in range(4):
                    dve.wait_ge(s_ok, h * 4 + (i + 1))
                    st.step(dve.tensor_reduce(smx[:, 3, i:i + 1], bank[4 + i][:], AX.X, ALU.max))
                    st.wait()
                    dve.tensor_scalar(smx[:, 0, i:i + 1], smx[:, 3, i:i + 1], -(A_D ** -0.5), None, ALU.mult)\
                        .then_inc(max_ok, 1)
                for t in range(2):
                    s0, s1 = smx[:, 2, 2 * t:2 * t + 1], smx[:, 2, 2 * t + 1:2 * t + 2]
                    dve.wait_ge(p_ok, h * 4 + (2 * t + 2))
                    st.step(dve.reciprocal(smx[:, 2, 2 * t:2 * t + 2], smx[:, 1, 2 * t:2 * t + 2]))
                    st.wait()
                    st.step(dve.tensor_tensor(s1, s1, lam[:, 3:4], ALU.mult))
                    st.wait()
                    st.step(dve.tensor_scalar(probs[:, t, 1], probs[:, t, 1], s1, None, ALU.mult))
                    st.wait()
                    dve.scalar_tensor_tensor(probs[:, t, 0], probs[:, t, 0], s0, probs[:, t, 1], ALU.mult,
                                             ALU.subtract).then_inc(a_ok, 1)
                for b in range(2):
                    dve.wait_ge(at_t, h * 2 + (b + 1))
                    dve.tensor_copy(flat(aT[:, 2 * b:2 * b + 2]), bank[4 + b][:]).then_inc(aT_ok, 1)
                dve.wait_ge(pv_ok, h + 1)
                st.step(dve.tensor_copy(flat(o1), bank[6][:]))
                st.wait()
                squares(q_u, o1, 2)
                inverse_rms(h * 3 + (BATCH + 3), 2, A_DV)
                dve.wait_ge(g_ok, h + 1)
                for t in range(2):
                    dve.scalar_tensor_tensor(u1[:, t, bass.ds(h * A_DV, A_DV)], o1[:, t], stat[:, 2, t:t + 1],
                                             silu_ag[:, t], ALU.mult, ALU.mult).then_inc(u_ok, 1)

            keys(0)
            queries(0)
            with dve.Fori(1, A_HEADS) as h:
                st.enter(h - 1, 33)
                attend(h - 1)
                keys(h)
                queries(h)
                st.leave(A_HEADS - 1)
            attend(A_HEADS - 1)

            dve.wait_ge(u_ok, NT * G_HEADS + 2 * A_HEADS)
            gate_rows(5, 0, 8)
            activation_tiles(3, hfu, weighted(V_SUB, A_DV // P, 2 * P), 2 * P)
            def result(j, first):
                if not first:
                    dve.wait_ge(y_out, j * 32)
                for t in range(2):
                    complete(j + (3 * DIFF + 4 * A_HEADS), j + OUT1, t, 2)
                    dve.tensor_tensor(yrow[:, t], bank[t][:], gate_row[:, 0, bass.ds(j * CW, CW)], ALU.mult)\
                        .then_inc(freed[t], 1)
                    dve.wait_ge(freed[t], j + (OUT1 + 1))
                    dve.tensor_tensor(yrow[:, t], yrow[:, t], u[:, t, bass.ds(j * CW, CW)], ALU.add)\
                        .then_inc(y_ok, 1)

            result(0, True)
            with dve.Fori(1, 4) as j:
                result(j, False)


INPUTS = ("x", "c", "ctx", "c_ctx", "norm_w", "ada_w", "ada_b", "gla_w_in", "gla_gate_a1", "gla_gate_a2",
          "gla_gate_b", "gla_gn_w", "gla_w_out", "diff_w_in", "diff_qn_w", "diff_kn_w", "diff_lam",
          "diff_subln_w", "diff_w_out")


def constants():
    n = 2 * P
    row = np.repeat(np.arange(n // GRID_W), GRID_W).astype(np.float32)
    col = np.tile(np.arange(GRID_W), n // GRID_W).astype(np.float32)
    half = A_D // 2
    freq = (np.float32(ROPE_BASE) ** (-np.arange(0, half, 2, dtype=np.float32) / np.float32(half))).astype(np.float32)
    ang = np.concatenate([row[:, None] * freq] * 2 + [col[:, None] * freq] * 2, axis=1)
    sign = np.tile(np.repeat(np.float32([-1, 1]), A_D // 4), 2)
    j, i = np.arange(P)[:, None], np.arange(P)[None, :]
    return {
        "cos": np.tile(np.cos(ang), (1, 2)).astype(np.float32),
        "sin": np.tile(np.sin(ang) * sign, (1, 2)).astype(np.float32),
        "ident": np.eye(P, dtype=np.float32),
        "mask1": ((j <= i) | ((j >= HALF) & (i < HALF))).astype(np.int32),
        "mask2": ((j % HALF) >= np.arange(HALF)[None, :]).astype(np.int32),
    }


def kernel(**inputs):
    import concourse.bacc as bacc
    from concourse.bass_utils import run_bass_kernel_spmd

    nc = bacc.Bacc("TRN2", target_bir_lowering=False, num_devices=1)
    arrays, io = {}, {}
    for name, a in list((n, inputs[n]) for n in INPUTS) + list(constants().items()):
        a = np.ascontiguousarray(a)
        arrays[f"in_{name}"] = a
        io[name] = nc.dram_tensor(f"in_{name}", a.shape, mybir.dt.from_np(a.dtype), kind="ExternalInput").ap()
    out = nc.dram_tensor("result", (1, 2 * P, D), F32, kind="ExternalOutput").ap()
    build(nc, io, out)
    return run_bass_kernel_spmd(nc, [arrays], core_ids=[0]).results[0]["result"]
```
